# Optimizing a Trainium2 kernel written in Bass

```python
import math
import jax, jax.numpy as jnp
from jax import lax
import numpy as np

D_MODEL = 2048
BATCH = 1
SEQ = 256
DEPTH = 1

HEAD_DIM = 64
SWA_Q_HEADS = D_MODEL // (2 * HEAD_DIM)
SWA_KV_HEADS = max(1, SWA_Q_HEADS // 8)
SWA_GROUP = SWA_Q_HEADS // SWA_KV_HEADS
SWA_WINDOW = 128
SWA_BLOCK = 128
MOBA_HEADS = D_MODEL // (2 * HEAD_DIM)
MOBA_BLOCK = 256
MOBA_TOPK = 3
MOBA_Q_CHUNK = 32
N_HEADS = SWA_Q_HEADS + MOBA_HEADS
D_SWA = SWA_Q_HEADS * HEAD_DIM
D_SWA_KV = SWA_KV_HEADS * HEAD_DIM
D_MOBA = MOBA_HEADS * HEAD_DIM
D_MIX = D_SWA + D_MOBA
D_QKV = D_SWA + 2 * D_SWA_KV + 3 * D_MOBA
SPLIT_POINTS = [D_SWA, D_SWA + D_SWA_KV, D_SWA + 2 * D_SWA_KV,
                D_SWA + 2 * D_SWA_KV + D_MOBA, D_SWA + 2 * D_SWA_KV + 2 * D_MOBA]
REL_BUCKETS = 32
REL_MAX_DISTANCE = 2048
N_GROUPS = 4
EXPERTS_PER_GROUP = 8
N_EXPERTS = N_GROUPS * EXPERTS_PER_GROUP
D_EXPERT = 512
EXPERT_TOPK = 2
EPS = 1e-6
NEG = -1e30
SCALE = 1.0 / math.sqrt(HEAD_DIM)

kernel_name = 'hybrid_swa_sink_moba_hmoe_adaln'

def rmsnorm(x, g):
    x32 = x.astype(jnp.float32)
    r = lax.rsqrt(jnp.mean(x32 * x32, axis=-1, keepdims=True) + EPS)
    return (x32 * r).astype(x.dtype) * g

def rel_bucket(dist):
    n = jnp.maximum(dist, 0)
    max_exact = REL_BUCKETS // 2
    nf = jnp.maximum(n, 1).astype(jnp.float32)
    large = max_exact + (jnp.log(nf / max_exact) / math.log(REL_MAX_DISTANCE / max_exact)
                         * (REL_BUCKETS - max_exact)).astype(jnp.int32)
    large = jnp.minimum(large, REL_BUCKETS - 1)
    return jnp.where(n < max_exact, n, large)

def sliding_window_attention(q, k, v, sinks, rel_bias_a):
    b, s = q.shape[0], q.shape[1]
    w = SWA_BLOCK
    nblk = s // w
    qb = q.reshape(b, nblk, w, SWA_KV_HEADS, SWA_GROUP, HEAD_DIM)

    def with_prev(t):
        tb = t.reshape(b, nblk, w, SWA_KV_HEADS, HEAD_DIM)
        prev = jnp.pad(tb, ((0, 0), (1, 0), (0, 0), (0, 0), (0, 0)))[:, :-1]
        return jnp.concatenate([prev, tb], axis=2)

    kc, vc = with_prev(k), with_prev(v)
    scores = jnp.einsum('bnqkgd,bnskd->bnkgqs', qb, kc).astype(jnp.float32) * SCALE
    kidx = jnp.arange(2 * w)
    dist = (w + jnp.arange(w))[:, None] - kidx[None, :]
    band = (dist >= 0) & (dist < SWA_WINDOW)
    start_ok = (jnp.arange(nblk)[:, None] * w - w + kidx[None, :]) >= 0
    valid = band[None] & start_ok[:, None, :]
    bias = rel_bias_a[rel_bucket(dist)].astype(jnp.float32)
    bias = jnp.transpose(bias, (2, 0, 1)).reshape(SWA_KV_HEADS, SWA_GROUP, w, 2 * w)
    logits = jnp.where(valid[None, :, None, None], scores + bias, NEG)
    sink = sinks.astype(jnp.float32).reshape(SWA_KV_HEADS, SWA_GROUP)[None, None, :, :, None, None]
    m = jnp.maximum(jnp.max(logits, axis=-1, keepdims=True), sink)
    e = jnp.exp(logits - m)
    p = e / (jnp.sum(e, axis=-1, keepdims=True) + jnp.exp(sink - m))
    out = jnp.einsum('bnkgqs,bnskd->bnqkgd', p.astype(v.dtype), vc)
    return out.reshape(b, s, D_SWA)

def moba_attention(q, k, v, rel_bias_b):
    b, s = q.shape[0], q.shape[1]
    nblk = -(-s // MOBA_BLOCK)
    s_pad = nblk * MOBA_BLOCK
    pad = ((0, 0), (0, s_pad - s), (0, 0), (0, 0))
    q, k, v = [jnp.transpose(jnp.pad(t, pad), (0, 2, 1, 3)) for t in (q, k, v)]
    kblk = k.reshape(b, MOBA_HEADS, nblk, MOBA_BLOCK, HEAD_DIM)
    vblk = v.reshape(b, MOBA_HEADS, nblk, MOBA_BLOCK, HEAD_DIM)
    kmean = jnp.mean(kblk.astype(jnp.float32), axis=3)
    gate = jnp.einsum('bhtd,bhnd->bhtn', q.astype(jnp.float32), kmean)
    cur = jnp.arange(s_pad) // MOBA_BLOCK
    past = jnp.arange(nblk)[None, :] < cur[:, None]
    gate = jnp.where(past, gate, NEG)
    n_sel = min(MOBA_TOPK, nblk)
    _, sel = lax.top_k(gate, n_sel)
    sel_ok = sel < cur[:, None]
    tab = rel_bias_b.T.astype(jnp.float32)
    n_chunk = s_pad // MOBA_Q_CHUNK

    def chunk_major(t):
        return jnp.moveaxis(t.reshape(b, MOBA_HEADS, n_chunk, MOBA_Q_CHUNK, *t.shape[3:]), 2, 0)

    xs = (chunk_major(q), chunk_major(sel), chunk_major(sel_ok),
          jnp.arange(n_chunk, dtype=jnp.int32) * MOBA_Q_CHUNK)
    bi = jnp.arange(b)[:, None, None, None]
    hi = jnp.arange(MOBA_HEADS)[None, :, None, None]
    pidx = jnp.arange(MOBA_BLOCK)

    def step(args):
        qc, selc, okc, t0 = args
        tq = t0 + jnp.arange(MOBA_Q_CHUNK)
        ksel = kblk[bi, hi, selc]
        vsel = vblk[bi, hi, selc]
        s_sel = jnp.einsum('bhqd,bhqjpd->bhqjp', qc, ksel).astype(jnp.float32) * SCALE
        kpos = selc[..., None] * MOBA_BLOCK + pidx
        bias_sel = tab[hi[..., None], rel_bucket(tq[None, None, :, None, None] - kpos)]
        s_sel = jnp.where(okc[..., None], s_sel + bias_sel, NEG)
        own0 = (t0 // MOBA_BLOCK) * MOBA_BLOCK
        kown = lax.dynamic_slice_in_dim(k, own0, MOBA_BLOCK, axis=2)
        vown = lax.dynamic_slice_in_dim(v, own0, MOBA_BLOCK, axis=2)
        s_own = jnp.einsum('bhqd,bhpd->bhqp', qc, kown).astype(jnp.float32) * SCALE
        dist = tq[:, None] - (own0 + pidx)[None, :]
        s_own = jnp.where(dist >= 0, s_own + tab[:, rel_bucket(dist)], NEG)
        logits = jnp.concatenate([s_sel.reshape(b, MOBA_HEADS, MOBA_Q_CHUNK, n_sel * MOBA_BLOCK), s_own], axis=-1)
        p = jax.nn.softmax(logits, axis=-1).astype(v.dtype)
        p_sel = p[..., :n_sel * MOBA_BLOCK].reshape(b, MOBA_HEADS, MOBA_Q_CHUNK, n_sel, MOBA_BLOCK)
        p_own = p[..., n_sel * MOBA_BLOCK:]
        return (jnp.einsum('bhqjp,bhqjpd->bhqd', p_sel, vsel)
                + jnp.einsum('bhqp,bhpd->bhqd', p_own, vown))

    out = lax.map(step, xs)
    out = jnp.moveaxis(out, 0, 2).reshape(b, MOBA_HEADS, s_pad, HEAD_DIM)[:, :, :s]
    return jnp.transpose(out, (0, 2, 1, 3)).reshape(b, s, D_MOBA)

def hier_moe(h, w_group, b_group, w_router, b_router, w_gate, w_up, w_down):
    b, s, d = h.shape
    ht = h.reshape(b * s, d)
    grp_logits = (ht @ w_group).astype(jnp.float32) + b_group
    grp_prob = jax.nn.softmax(grp_logits, axis=-1)
    p_grp, g_idx = lax.top_k(grp_prob, 1)
    exp_logits = ((ht @ w_router).astype(jnp.float32) + b_router).reshape(-1, N_GROUPS, EXPERTS_PER_GROUP)
    in_grp = jnp.take_along_axis(exp_logits, g_idx[:, :, None], axis=1)[:, 0]
    top_val, top_idx = lax.top_k(in_grp, EXPERT_TOPK)
    wts = p_grp * jax.nn.softmax(top_val, axis=-1)
    e_idx = g_idx * EXPERTS_PER_GROUP + top_idx
    gates = jnp.sum(jax.nn.one_hot(e_idx, N_EXPERTS, dtype=jnp.float32) * wts[..., None], axis=1).astype(ht.dtype)
    out = jnp.zeros_like(ht)
    for e in range(N_EXPERTS):
        hid = jax.nn.silu(ht @ w_gate[e]) * (ht @ w_up[e])
        out = out + gates[:, e:e + 1] * (hid @ w_down[e])
    return out.reshape(b, s, d)

def setup_inputs(seed: int = 0) -> dict:
    key = jax.random.key(seed)
    ks = jax.random.split(key, 20)

    def nrm(k, shape, scale):
        return jax.random.normal(k, shape, jnp.float32) * scale

    d = D_MODEL
    return {
        'x': nrm(ks[0], (BATCH, SEQ, d), 1.0),
        'c': nrm(ks[1], (BATCH, d), 1.0),
        'rel_bias': nrm(ks[2], (REL_BUCKETS, N_HEADS), 0.5),
        'w_ada': nrm(ks[3], (DEPTH, d, 6 * d), 0.5 * d ** -0.5),
        'b_ada': nrm(ks[4], (DEPTH, 6 * d), 0.1),
        'norm1_g': 1.0 + nrm(ks[5], (DEPTH, d), 0.02),
        'norm2_g': 1.0 + nrm(ks[6], (DEPTH, d), 0.02),
        'w_qkv': nrm(ks[7], (DEPTH, d, D_QKV), d ** -0.5),
        'attn_sinks': nrm(ks[8], (DEPTH, SWA_Q_HEADS), 0.5),
        'swa_out_g': 1.0 + nrm(ks[9], (DEPTH, D_SWA), 0.02),
        'moba_out_g': 1.0 + nrm(ks[10], (DEPTH, D_MOBA), 0.02),
        'w_o': nrm(ks[11], (DEPTH, D_MIX, d), D_MIX ** -0.5),
        'w_group': nrm(ks[12], (DEPTH, d, N_GROUPS), d ** -0.5),
        'b_group': nrm(ks[13], (DEPTH, N_GROUPS), 0.01),
        'w_expert_router': nrm(ks[14], (DEPTH, d, N_EXPERTS), d ** -0.5),
        'b_expert_router': nrm(ks[15], (DEPTH, N_EXPERTS), 0.01),
        'w_gate': nrm(ks[16], (DEPTH, N_EXPERTS, d, D_EXPERT), d ** -0.5),
        'w_up': nrm(ks[17], (DEPTH, N_EXPERTS, d, D_EXPERT), d ** -0.5),
        'w_down': nrm(ks[18], (DEPTH, N_EXPERTS, D_EXPERT, d), D_EXPERT ** -0.5),
        'final_g': 1.0 + nrm(ks[19], (d,), 0.02),
    }

def reference(x, c, rel_bias, w_ada, b_ada, norm1_g, norm2_g, w_qkv, attn_sinks, swa_out_g,
              moba_out_g, w_o, w_group, b_group, w_expert_router, b_expert_router,
              w_gate, w_up, w_down, final_g):
    b, s, _ = x.shape
    c_act = jax.nn.silu(c)
    bias_swa = rel_bias[:, :SWA_Q_HEADS]
    bias_moba = rel_bias[:, SWA_Q_HEADS:]
    for l in range(DEPTH):
        mod = c_act @ w_ada[l] + b_ada[l]
        sh1, sc1, g1, sh2, sc2, g2 = [m[:, None, :] for m in jnp.split(mod, 6, axis=-1)]
        h = rmsnorm(x, norm1_g[l]) * (1 + sc1) + sh1
        qkv = h @ w_qkv[l]
        q_a, k_a, v_a, q_b, k_b, v_b = jnp.split(qkv, SPLIT_POINTS, axis=-1)
        y_a = sliding_window_attention(
            q_a.reshape(b, s, SWA_Q_HEADS, HEAD_DIM),
            k_a.reshape(b, s, SWA_KV_HEADS, HEAD_DIM),
            v_a.reshape(b, s, SWA_KV_HEADS, HEAD_DIM),
            attn_sinks[l], bias_swa)
        y_b = moba_attention(
            q_b.reshape(b, s, MOBA_HEADS, HEAD_DIM),
            k_b.reshape(b, s, MOBA_HEADS, HEAD_DIM),
            v_b.reshape(b, s, MOBA_HEADS, HEAD_DIM),
            bias_moba)
        y = jnp.concatenate([rmsnorm(y_a, swa_out_g[l]), rmsnorm(y_b, moba_out_g[l])], axis=-1) @ w_o[l]
        x = x + g1 * y
        h = rmsnorm(x, norm2_g[l]) * (1 + sc2) + sh2
        x = x + g2 * hier_moe(h, w_group[l], b_group[l], w_expert_router[l], b_expert_router[l],
                              w_gate[l], w_up[l], w_down[l])
    return rmsnorm(x, final_g)


_drawn_inputs = setup_inputs


def setup_inputs(seed=0):
    import zlib

    import numpy as np

    out = dict(_drawn_inputs(seed))
    spreads = {}
    factors = {'norm1_g': 6.597,
     'norm2_g': 4.979,
     'attn_sinks': 8.0,
     'swa_out_g': 8.0,
     'moba_out_g': 8.0,
     'b_group': 8.0,
     'b_expert_router': 27.238,
     'final_g': 8.372}
    for name, (base, spread) in spreads.items():
        noise = np.random.default_rng([zlib.crc32(name.encode()), seed]).standard_normal(out[name].shape)
        drawn = base * np.exp(spread * noise) if base else spread * noise
        out[name] = __import__('jax').numpy.asarray(drawn.astype(out[name].dtype))
    for name, factor in factors.items():
        out[name] = (out[name] * factor).astype(out[name].dtype)
    return out
```

```python
import math
from contextlib import ExitStack

import numpy as np
import concourse.bass as bass
from concourse import mybir

F32 = mybir.dt.float32
I32 = mybir.dt.int32
ALU = mybir.AluOpType
ACT = mybir.ActivationFunctionType
AX = mybir.AxisListType

P = 128
D = 2048
T = 256
H = T // P
KT = D // P
HD = 64
NHA, NHB = 16, 16
NH = NHA + NHB
KVA = 2
WINDOW = 128
BUCKETS = 32
MAX_DIST = 2048
G, EPG = 4, 8
E = G * EPG
FE = 512
NR = G + E
SLOTS = 64
EPS = 1e-6
NEG = -1e30
LOW = -3.0e38
SCALE = 1.0 / math.sqrt(HD)

RING = 8
SLOT = 4096
CW = 256
QKV_CHUNKS = (NHA * HD + 2 * KVA * HD + 3 * NHB * HD) // CW
WO_CHUNKS = D // CW
ADA_CHUNKS = KT // 2
SH1, SC1, G1, SH2, SC2, G2 = range(6)
UL = 384
EXP_CHUNKS = 6


def rel_bucket(dist):
    n = np.maximum(dist, 0)
    exact = BUCKETS // 2
    nf = np.maximum(n, 1).astype(np.float32)
    large = exact + (np.log(nf / np.float32(exact)) / np.float32(math.log(MAX_DIST / exact))
                     * np.float32(BUCKETS - exact)).astype(np.int32)
    return np.where(n < exact, n, np.minimum(large, BUCKETS - 1))


C_ID, C_TRI, C_ONE = 0, P, 2 * P
C_IOTA = 3 * P
C_DG = C_IOTA + SLOTS
C_DE = C_DG + G
C_REV = C_DE + EPG
C_N = C_REV + P


def constants():
    c = np.zeros((P, C_N), np.float32)
    c[:, C_ID:C_ID + P] = np.eye(P)
    c[:, C_TRI:C_TRI + P] = np.triu(np.ones((P, P)), 1)
    c[:, C_ONE:C_ONE + P] = 1.0
    c[:, C_IOTA:C_IOTA + SLOTS] = np.arange(SLOTS)
    c[:, C_DG:C_DG + G] = np.arange(G, 0, -1)
    c[:, C_DE:C_DE + EPG] = np.arange(EPG, 0, -1)
    c[:, C_REV:C_REV + P] = np.eye(P)[::-1]
    dist = 255 - np.arange(UL)
    line = np.zeros((BUCKETS, 2 * UL), np.float32)
    line[rel_bucket(dist), np.arange(UL)] = (dist >= 0)
    bad = np.zeros((NH, UL), np.float32)
    bad[:NHA, (dist < 0) | (dist >= WINDOW)] = NEG
    bad[NHA:, dist < 0] = NEG
    line[:, UL:] = bad
    return c, line


def stream_plan():
    order = [("ada", (part, j), "pe") for part in (SH1, SC1) for j in range(ADA_CHUNKS)]
    vec = [("adv", (part, j), "dve") for part in (G1, SH2, SC2) for j in range(ADA_CHUNKS)]
    done = 0
    for c in range(QKV_CHUNKS):
        order.append(("qkv", c, "pe"))
        upto = min(len(vec), (c + 1) * len(vec) // (QKV_CHUNKS - 2))
        order += vec[done:upto]
        done = upto
    order += [("bias", 0, "bias"), ("bias", 1, "bias"), ("x", 0, "x")]
    for c in range(WO_CHUNKS):
        order += [("wo", c, "pe"), ("adv", (G2, c), "dve")]
    number = {(k, i): n for n, (k, i, _) in enumerate(order)}
    seen, free = {}, []
    for _, _, who in order:
        seen[who] = seen.get(who, 0) + 1
        free.append((who, seen[who]))
    return order, number, free


def layer_kernel(nc, x, c, rel_bias, w_ada, b_ada, norm1_g, norm2_g, w_qkv, attn_sinks, swa_out_g,
                 moba_out_g, w_o, w_group, b_group, w_router, b_router, w_gate, w_up, w_down,
                 final_g, cst_d, line_d, out):
    order, number, free_at = stream_plan()
    N0 = len(order)
    PE0 = sum(who == "pe" for _, _, who in order)
    assert N0 % 2 == 0
    S0 = N0 % RING

    x_v = x[0].rearrange("(h p) n -> p h n", p=P)
    out_v = out[0].rearrange("(h p) n -> p h n", p=P)
    ada_v = w_ada[0].rearrange("(p t) n -> p t n", t=KT)
    qkv_v = w_qkv[0].rearrange("(p t) n -> p t n", t=KT)
    wo_v = w_o[0].rearrange("(t p) n -> p t n", p=P)
    gate_v = w_gate[0].rearrange("e (p t) n -> e p t n", t=KT)
    up_v = w_up[0].rearrange("e (p t) n -> e p t n", t=KT)
    down_v = w_down[0].rearrange("e (k p) n -> e p k n", p=P)
    u_scr = nc.dram_tensor("u_scr", [NH, UL], F32, kind="Internal").ap()
    m_scr = nc.dram_tensor("m_scr", [6, D], F32, kind="Internal").ap()

    with ExitStack() as ctx:
        def sb(name, n, dt=F32):
            return ctx.enter_context(nc.sbuf_tensor(name, [P, n], dt))

        def sem(name):
            return ctx.enter_context(nc.semaphore(name))

        ring = sb("ring", RING * SLOT)
        r1 = sb("r1", H * D)
        r2 = sb("r2", H * D)
        r3 = sb("r3", H * D)
        W = sb("W", 6400)
        cst = sb("cst", C_N)
        gy = sb("gy", H * CW)
        idr = sb("idr", H * P)
        sq = sb("sq", 2 * T)
        sm = sb("sm", 640)
        ovi = sb("ovi", 1, I32)
        PS = ctx.enter_context(nc.psum_tensor("PS", [P, 8, 512], F32))

        def slot(s):
            return ring[:, s * SLOT:(s + 1) * SLOT]

        x1 = r1[:, :].rearrange("p (h n) -> p h n", h=H)
        qT = r1[:, :].rearrange("p (b t) -> p b t", t=T)
        hT = r2[:, :].rearrange("p (k t) -> p k t", t=T)
        yT = hT
        kTb = r3[:, :].rearrange("p (b t) -> p b t", t=T)
        h2T = kTb
        acc = r3[:, :].rearrange("p (h n) -> p h n", h=H)
        g2b, fgb = r2[:, 0:D], r2[:, D:2 * D]
        VW = (KVA + NHB) * HD
        v_sb = W[:, 0:H * VW].rearrange("p (h n) -> p h n", h=H)
        o = H * VW
        kTa = W[:, o:o + 2 * KVA * T].rearrange("p (b t) -> p b t", t=T)
        o += 2 * KVA * T
        L = W[:, o:o + 4 * 384].rearrange("p (b t) -> p b t", b=4)
        PT = W[:, o + 4 * 384:o + 8 * 384].rearrange("p (b t) -> p b t", b=4)
        ada_acc = W[:, o:o + D]
        mrow = W[:, o + D:o + D + 512]
        brow = W[:, o + D + 512:o + D + 1024]
        line = W[0:NH, o:o + 2 * UL]
        relb = W[0:BUCKETS, o + 2 * UL:o + 2 * UL + NH]
        u_sb = W[0:NH, o + 2 * UL + NH:o + 3 * UL + NH]
        g1b = W[:, 0:D]
        wr = W[:, o - 4 * T:o - 4 * T + KT * NR].rearrange("p (t n) -> p t n", n=NR)
        lgT = W[0:NR, o - 4 * T + KT * NR:o - 4 * T + KT * NR + T]
        RT0 = o
        yd = W[:, 0:D]
        EQ = W[:, 2048:2560].rearrange("p (h n) -> p h n", h=H)
        selr = W[:, 2560:3072].rearrange("p (h n) -> p h n", h=H)
        selg = W[:, 3072:3584].rearrange("p (h n) -> p h n", h=H)
        selT = W[:, 3584:3840]
        ex, den, rc, sg, hid = [W[:, 3840 + T * i:3840 + T * (i + 1)] for i in range(5)]
        hidT = W[:, 5120:5376].rearrange("p (b n) -> p b n", b=2)
        junk = W[:, 0:D]

        ident = cst[:, C_ID:C_ID + P]
        rev = cst[:, C_REV:C_REV + P]
        tri = cst[:, C_TRI:C_TRI + P]
        ones = cst[:, C_ONE:C_ONE + P]
        iota = cst[:, C_IOTA:C_IOTA + SLOTS]

        at = [0]

        def small(n):
            at[0] += n
            assert at[0] <= 640
            return sm[:, at[0] - n:at[0]]

        ssum, rstd = small(H), small(H)
        cT, cE = small(KT), small(KT)
        g1T, g2T, goT = small(KT), small(KT), small(KT)
        A1, B1, A2, B2 = small(KT), small(KT), small(KT), small(KT)
        sink = small(NHA)
        nmx, psum_, rden = (small(NH * 2).rearrange("p (h t) -> p h t", t=2) for _ in range(3))
        esink = small(NHA * 2).rearrange("p (h t) -> p h t", t=2)
        part = small(H * WO_CHUNKS).rearrange("p (h c) -> p h c", h=H)
        posm, gates, over = (small(H * E).rearrange("p (h e) -> p h e", h=H) for _ in range(3))
        rb = W[:, RT0 - 4 * T + KT * NR + T:RT0 - 4 * T + KT * NR + T + NR]
        assert KT * NR + T + NR <= 4 * T
        rt_at = [RT0]

        def rt(*dims):
            n = int(np.prod(dims))
            v = W[:, rt_at[0]:rt_at[0] + n]
            rt_at[0] += n
            names = "abc"[:len(dims)]
            if len(dims) == 1:
                return v
            spec = "p (" + " ".join(names) + ") -> p " + " ".join(names)
            return v.rearrange(spec, **dict(zip(names, dims)))

        R_lg, R_goh, R_t4, R_ge, R_x = rt(H, NR), rt(H, G), rt(H, G), rt(H, G), rt(H, G, EPG)
        R_in, R_in2, R_o1, R_o2, R_t8 = (rt(H, EPG) for _ in range(5))
        R_gm, R_v1, R_v2, R_m, R_e2, R_w1 = (rt(H) for _ in range(6))
        R_mem = rt(H, E)
        F_h = slot(6).rearrange("p (k t) -> p k t", t=T)
        F_ex, F_hid, F_hT = (slot(7)[:, i * FE:(i + 1) * FE] for i in range(3))

        x_in, cst_in, small_in, line_in = sem("x_in"), sem("cst_in"), sem("small_in"), sem("line_in")
        landed = [sem(f"landed{s}") for s in range(RING)]
        pe_chunk = sem("pe_chunk")
        ab_ok = sem("ab_ok")
        brow_in = sem("brow_in")
        kz = sem("kz")
        u_ps, u_ok, u_out = sem("u_ps"), sem("u_ok"), sem("u_out")
        ss_ok, ms_ok, rt_ok, id_ok = sem("ss_ok"), sem("ms_ok"), sem("rt_ok"), sem("id_ok")
        tr_ps, tr_act, tr_dve = sem("tr_ps"), sem("tr_act"), sem("tr_dve")
        aff_act, aff_dve = sem("aff_act"), sem("aff_dve")
        silu_e, silu_c = sem("silu_e"), sem("silu_c")
        accd, mod_ps, mod_ok, mod_out, mod_in = sem("accd"), sem("mod_ps"), sem("mod_ok"), sem("mod_out"), sem("mod_in")
        qkv_ok = sem("qkv_ok")
        s_ps, lg_ok, nm_ok, p_ok, sum_ok = sem("s_ps"), sem("lg_ok"), sem("nm_ok"), sem("p_ok"), sem("sum_ok")
        pn_ok, pt_ps, pt_ok, y_ps, y_ok, sq_ok, yss_ps = (sem("pn_ok"), sem("pt_ps"), sem("pt_ok"), sem("y_ps"),
                                                          sem("y_ok"), sem("sq_ok"), sem("yss_ps"))
        yms_ok, yrt_ok, yn_ok = sem("yms_ok"), sem("yrt_ok"), sem("yn_ok")
        x1_ok, x1_ss, xr_ok = sem("x1_ok"), sem("x1_ss"), sem("xr_ok")
        rw_in = sem("rw_in")
        rl_ps, rl_ok, rt_ps, pos_ps, mem_ok, ge_in, ge_ok, e2_in, e2_ok = (
            sem("rl_ps"), sem("rl_ok"), sem("rt_ps"), sem("pos_ps"), sem("mem_ok"), sem("ge_in"),
            sem("ge_ok"), sem("e2_in"), sem("e2_ok"))
        routed = sem("routed")
        eq_ok, sel_ok = sem("eq_ok"), sem("sel_ok")
        ga_ps, hg_act, hg_dve = sem("ga_ps"), sem("hg_act"), sem("hg_dve")
        ex_ok, silu_st, hid_ok, hd_ps, hidT_ok = sem("ex_ok"), sem("silu_st"), sem("hid_ok"), sem("hd_ps"), sem("hidT_ok")
        st_ps, selT_ok, yd_ok, sc_ps, acc_ok = sem("st_ps"), sem("selT_ok"), sem("yd_ok"), sem("sc_ps"), sem("acc_ok")
        fb_in, fb_up, fb_ex, fb_hid, fb_tps, fb_tok, fb_dn, fb_acc, fb_ht, fb_hps, fb_link = (
            [sem(f"fb{i}") for i in range(11)])
        fin_in, f_ss, f_ms, f_rt, f_r, o_ok, o_out = (sem("fin_in"), sem("f_ss"), sem("f_ms"), sem("f_rt"),
                                                    sem("f_r"), sem("o_ok"), sem("o_out"))
        v_ch, a_ch = sem("v_ch"), sem("a_ch")

        def on_ring(eng, kind, i):
            n = number[kind, i]
            eng.wait_ge(landed[n % RING], 16 * (n // RING + 1))
            return slot(n % RING)

        def chain(eng, s):
            n = [0]

            def link(ins):
                n[0] += 1
                ins.then_inc(s, 1)
                eng.wait_ge(s, n[0])
            return link

        MADE = [SH1, SC1, G1, SH2, SC2, G2]
        SUM_AFTER = {}
        for i, pt_ in enumerate((G1, SH2, SC2)):
            n = number["adv", (pt_, ADA_CHUNKS - 1)]
            SUM_AFTER.setdefault(min([q for q in range(QKV_CHUNKS) if number["qkv", q] > n],
                                     default=QKV_CHUNKS - 1), []).append(pt_)
        NQ = NHA * HD // CW
        BQ, BK, BV = NQ + 1, NQ + 1 + NHB * HD // CW, NQ + 1 + 2 * NHB * HD // CW
        CPB = CW // P

        block = ctx.enter_context(nc.Block())

        @block.sync
        def _(sp):
            sp.dma_start(x1, x_v).then_inc(x_in, 16)

            def read_by(sp, who, count):
                s, each = {"pe": (pe_chunk, 1), "dve": (accd, 2), "bias": (lg_ok, NH // 2), "x": (xr_ok, 1)}[who]
                sp.wait_ge(s, each * count)

            def load(n, dst, src):
                if n >= RING:
                    who, count = free_at[n - RING]
                    read_by(sp, who, count)
                sp.dma_start(dst, src).then_inc(landed[n % RING], 16)

            for n, (kind, i, _) in enumerate(order):
                s = slot(n % RING)
                if kind in ("ada", "adv"):
                    src = ada_v[:, 2 * i[1]:2 * i[1] + 2, i[0] * D:(i[0] + 1) * D]
                    load(n, s.rearrange("p (t n) -> p t n", t=2), src)
                elif kind == "qkv":
                    load(n, s.rearrange("p (t n) -> p t n", t=KT), qkv_v[:, :, i * CW:(i + 1) * CW])
                elif kind == "bias":
                    if i == 0:
                        sp.wait_ge(u_out, 16)
                    src = bass.AP(u_scr.tensor, u_scr.offset + i * 16 * UL, [[1, P], [UL, 16], [1, T]])
                    load(n, s.rearrange("p (h k) -> p h k", h=16), src)
                elif kind == "x":
                    load(n, s.rearrange("p (h n) -> p h n", h=H), x_v)
                else:
                    load(n, s.rearrange("p (t n) -> p t n", t=KT), wo_v[:, :, i * CW:(i + 1) * CW])

            def expert_chunk(e, k, s):
                if k < 4:
                    v = (gate_v, up_v)[k % 2]
                    t0 = (k // 2) * (KT // 2)
                    return (slot(s).rearrange("p (t n) -> p t n", n=FE), v[e, :, t0:t0 + KT // 2, :])
                return (slot(s).rearrange("p (t n) -> p t n", n=D), down_v[e, :, 2 * (k - 4):2 * (k - 4) + 2, :])

            for m in range(RING):
                who, count = free_at[N0 + m - RING]
                read_by(sp, who, count)
                dst, src = expert_chunk(m // EXP_CHUNKS, m % EXP_CHUNKS, (S0 + m) % RING)
                sp.dma_start(dst, src).then_inc(landed[(S0 + m) % RING], 16)

            for m in range(RING, EXP_CHUNKS * E):
                sp.wait_ge(pe_chunk, PE0 + m - RING + 1)
                dst, src = expert_chunk(m // EXP_CHUNKS, m % EXP_CHUNKS, (S0 + m) % RING)
                sp.dma_start(dst, src).then_inc(landed[(S0 + m) % RING], 16)

            sp.wait_ge(pe_chunk, PE0 + EXP_CHUNKS * E)
            sp.wait_ge(routed, 1)
            n_over = sp.value_load(ovi[0:1, 0:1], min_val=0, max_val=1)
            with sp.If(n_over > 0):
                with sp.Fori(0, E) as e:
                    sp.wait_ge(fb_dn, 8 * e + 1)
                    for k in range(4):
                        v = (gate_v, up_v)[k % 2]
                        t0 = (k // 2) * (KT // 2)
                        sp.dma_start(slot(k).rearrange("p (t n) -> p t n", n=FE),
                                     v[e, :, t0:t0 + KT // 2, :]).then_inc(fb_in, 16)
                    for k in range(2):
                        sp.dma_start(slot(4 + k).rearrange("p (t n) -> p t n", n=D),
                                     down_v[e, :, 2 * k:2 * k + 2, :]).then_inc(fb_in, 16)
            for h in range(H):
                sp.wait_ge(o_ok, h + 1)
                sp.dma_start(out_v[:, h, :], x1[:, h, :]).then_inc(o_out, 16)
            sp.wait_ge(o_out, 16 * H)

        @block.gpsimd
        def _(pool):
            pool.dma_start(cst[:, :], cst_d).then_inc(cst_in, 16)
            pool.dma_start(cT, c[0].rearrange("(p t) -> p t", t=KT)).then_inc(small_in, 16)
            pool.dma_start(line, line_d).then_inc(line_in, 16)
            pool.dma_start(relb, rel_bias).then_inc(line_in, 16)
            pool.dma_start(g1T, norm1_g[0].rearrange("(p t) -> p t", t=KT)).then_inc(small_in, 16)
            pool.dma_start(g2T, norm2_g[0].rearrange("(p t) -> p t", t=KT)).then_inc(small_in, 16)
            with nc.allow_non_contiguous_dma(reason="two vectors of 4 KiB"):
                for i, v in enumerate((swa_out_g, moba_out_g)):
                    pool.dma_start(goT[:, i * KT // 2:(i + 1) * KT // 2],
                                   v[0].rearrange("(b p) -> p b", p=P)).then_inc(small_in, 16)
            pool.dma_start(sink, bass.AP(attn_sinks.tensor, attn_sinks.offset, [[0, P], [1, NHA]])).then_inc(small_in, 16)
            nc.gpsimd.memset(r3[:, :], 0.0).then_inc(kz, 1)
            nc.gpsimd.memset(W[:, H * VW:H * VW + 2 * KVA * T], 0.0).then_inc(kz, 1)
            pool.wait_ge(u_ok, 1)
            pool.dma_start(u_scr, u_sb).then_inc(u_out, 16)
            for i, pt_ in enumerate(MADE):
                if i == 0:
                    pool.wait_ge(u_out, 16)
                else:
                    pool.wait_ge(mod_ok, i)
                if pt_ == G2:
                    pool.wait_ge(y_ok, NH // 2)
                    pool.dma_start(g1b, bass.AP(m_scr.tensor, m_scr.offset + G1 * D, [[0, P], [1, D]])).then_inc(mod_in, 16)
                    pool.dma_start(wr[:, :, 0:G], w_group[0].rearrange("(p t) n -> p t n", t=KT)).then_inc(rw_in, 16)
                    pool.dma_start(wr[:, :, G:NR], w_router[0].rearrange("(p t) n -> p t n", t=KT)).then_inc(rw_in, 16)
                    pool.dma_start(rb[:, 0:G], bass.AP(b_group.tensor, b_group.offset, [[0, P], [1, G]])).then_inc(rw_in, 16)
                    pool.dma_start(rb[:, G:NR], bass.AP(b_router.tensor, b_router.offset, [[0, P], [1, E]])).then_inc(rw_in, 16)
                pool.dma_start(brow, bass.AP(b_ada.tensor, b_ada.offset + pt_ * D, [[512, 4], [0, 32], [1, 512]])
                               ).then_inc(brow_in, 16)
                pool.wait_ge(mod_ok, i + 1)
                rows = bass.AP(mrow.tensor, mrow.offset, [[mrow.ap[0][0] * 32, 4], [1, 512]])
                pool.dma_start(m_scr[pt_].rearrange("(q n) -> q n", q=4), rows).then_inc(mod_out, 16)
                pool.wait_ge(mod_out, 16 * (i + 1))
                if pt_ not in (G1, G2):
                    dst = {SH1: B1, SC1: A1, SH2: B2, SC2: A2}[pt_]
                    pool.dma_start(dst, m_scr[pt_].rearrange("(p t) -> p t", t=KT)).then_inc(mod_in, 16)
            pool.wait_ge(rl_ps, 1)
            nc.gpsimd.memset(r3[:, :], 0.0).then_inc(acc_ok, 1)
            pool.wait_ge(pe_chunk, PE0 + EXP_CHUNKS * (E - 1) + 4)
            pool.dma_start(g2b, bass.AP(m_scr.tensor, m_scr.offset + G2 * D, [[0, P], [1, D]])).then_inc(fin_in, 16)
            pool.dma_start(fgb, bass.AP(final_g.tensor, final_g.offset, [[0, P], [1, D]])).then_inc(fin_in, 16)

        @block.scalar
        def _(act):
            A = nc.scalar
            act.wait_ge(small_in, 16 * 6)
            A.activation(cE, cT, ACT.Exp, scale=-1.0).then_inc(silu_e, 1)
            act.wait_ge(x_in, 16)
            for h in range(H):
                if h:
                    act.wait_ge(ss_ok, h)
                A.activation(junk, x1[:, h, :], ACT.Square, accum_out=ssum[:, h:h + 1]).then_inc(ss_ok, 1)
            act.wait_ge(ms_ok, 1)
            A.activation(rstd, rstd, ACT.Sqrt).then_inc(rt_ok, 1)
            for i in range(0, KT // 2, 2):
                act.wait_ge(tr_ps, i + 1)
                A.activation(hT[:, 2 * i:2 * i + 2, :], PS[:, i % 4, :].rearrange("p (k t) -> p k t", k=2),
                             ACT.Copy).then_inc(tr_act, 1)
            act.wait_ge(ab_ok, 1)
            act.wait_ge(tr_act, KT // 4)
            act.wait_ge(tr_dve, KT // 4)
            for t in range(0, KT, 2):
                A.activation(hT[:, t, :], hT[:, t, :], ACT.Identity, scale=A1[:, t:t + 1],
                             bias=B1[:, t:t + 1]).then_inc(aff_act, 1)
            for cc in range(QKV_CHUNKS):
                act.wait_ge(pe_chunk, 2 * ADA_CHUNKS + cc + 1)
                ps = PS[:, cc % 4, :]
                ps2 = ps.rearrange("p (b t) -> p b t", b=2)
                if cc < NQ or BQ <= cc < BK:
                    b0 = cc * CPB if cc < NQ else NHA // 2 + (cc - BQ) * CPB
                    back = bass.AP(ps.tensor, ps.offset + P - 1, [list(ps.ap[0]), [P, 2 * CPB], [-1, P]])
                    A.activation(qT[:, b0:b0 + CPB, :].rearrange("p b (h t) -> p (b h) t", h=H), back, ACT.Copy,
                                 scale=SCALE).then_inc(qkv_ok, 1)
                elif cc == NQ:
                    act.wait_ge(kz, 2)
                    for g in range(KVA):
                        for r in range(2):
                            A.activation(kTa[64 * r:64 * r + 64, 2 * g + r, :], ps[64 * g:64 * g + 64, 0:T], ACT.Copy)
                    A.activation(v_sb[:, :, 0:P], ps[:, T:2 * T].rearrange("p (h n) -> p h n", h=H),
                                 ACT.Copy).then_inc(qkv_ok, 1)
                elif cc < BV:
                    b0 = (cc - BK) * CPB
                    for r in range(2):
                        dst = kTb[64 * r:64 * r + 64, 2 * b0 + r:2 * b0 + r + 3:2, :]
                        last = A.activation(dst, ps2[64 * r:64 * r + 64], ACT.Copy)
                    last.then_inc(qkv_ok, 1)
                else:
                    n0 = P + (cc - BV) * CW
                    A.activation(v_sb[:, :, n0:n0 + CW], ps2, ACT.Copy).then_inc(qkv_ok, 1)

            def exps(h):
                act.wait_ge(nm_ok, h + 1)
                A.activation(L[:, h % 4, 0:T], L[:, h % 4, 0:T], ACT.Exp, bias=nmx[:, h, 0:1],
                             accum_out=psum_[:, h, 0:1])
                last = A.activation(L[:, h % 4, T:384], L[:, h % 4, T:384], ACT.Exp, bias=nmx[:, h, 1:2],
                                    accum_out=psum_[:, h, 1:2])
                if h < NHA:
                    last = A.activation(esink[:, h, :], nmx[:, h, :], ACT.Exp, bias=sink[:, h:h + 1])
                last.then_inc(p_ok, 1)

            def pt_evac(h):
                act.wait_ge(pt_ps, h + 1)
                if h >= 4:
                    act.wait_ge(y_ps, (h - 4) // 2 + 1)
                A.activation(PT[:, h % 4, :], PS[:, 2 + h % 2, 0:384], ACT.Copy).then_inc(pt_ok, 1)

            def squares(b):
                act.wait_ge(y_ok, b + 1)
                if b >= 2:
                    act.wait_ge(yss_ps, b - 1)
                A.activation(sq[:, b % 2 * T:(b % 2 + 1) * T], yT[:, b, :], ACT.Square).then_inc(sq_ok, 1)

            act.wait_ge(mod_out, 16 * 5)
            for h in range(NH + 3):
                if h < NH:
                    exps(h)
                if 1 <= h <= NH:
                    pt_evac(h - 1)
                if h >= 3 and h % 2 == 1:
                    squares((h - 3) // 2)
            act.wait_ge(yms_ok, 1)
            A.activation(sq[:, :], sq[:, :], ACT.Sqrt).then_inc(yrt_ok, 1)
            act.wait_ge(s_ps, NH)
            xs = on_ring(act, "x", 0)
            A.activation(r1[:, :], xs, ACT.Copy).then_inc(xr_ok, 1)
            for cc in range(WO_CHUNKS):
                act.wait_ge(x1_ok, cc + 1)
                for h in range(H):
                    last = A.activation(sq[:, h * CW:(h + 1) * CW], x1[:, h, cc * CW:(cc + 1) * CW],
                                        ACT.Square, accum_out=part[:, h, cc:cc + 1])
                last.then_inc(x1_ss, 1)
                if cc < WO_CHUNKS - 1:
                    act.wait_ge(x1_ss, cc + 1)
            act.wait_ge(ms_ok, 2)
            A.activation(rstd, rstd, ACT.Sqrt).then_inc(rt_ok, 1)
            act.wait_ge(ab_ok, 2)
            for i in range(0, KT // 2, 2):
                act.wait_ge(tr_ps, KT // 2 + i + 1)
                for r in range(2):
                    t = 2 * i + r
                    last = A.activation(h2T[:, t, :], PS[:, i % 4, r * T:(r + 1) * T], ACT.Identity,
                                        scale=A2[:, t:t + 1], bias=B2[:, t:t + 1])
                last.then_inc(tr_act, 1)
            act.wait_ge(rl_ps, 1)
            A.activation(lgT, PS[0:NR, 4, 0:T], ACT.Copy).then_inc(rl_ok, 1)
            act.wait_ge(ge_in, 1)
            A.activation(R_ge, R_ge, ACT.Exp).then_inc(ge_ok, 1)
            act.wait_ge(e2_in, 1)
            A.activation(R_e2, R_e2, ACT.Exp).then_inc(e2_ok, 1)

            def hg_evac(g):
                for i in range(0, KT // 2, 2):
                    act.wait_ge(ga_ps, 8 * g + i + 1)
                    for t in (2 * i, 2 * i + 1):
                        last = A.activation(hT[:, t, :], PS[:, 2, t % 2 * T:(t % 2 + 1) * T], ACT.Identity,
                                            scale=A2[:, t:t + 1], bias=B2[:, t:t + 1])
                    last.then_inc(hg_act, 1)

            def selT_evac(p):
                act.wait_ge(st_ps, p + 1)
                A.activation(selT, PS[:, 2, 0:T], ACT.Copy).then_inc(selT_ok, 1)

            with act.Fori(0, E // 4) as g:
                hg_evac(g)
                for i in range(4):
                    e = 4 * g + i
                    act.wait_ge(pe_chunk, PE0 + 4 + 24 * g + 6 * i)
                    A.activation(ex, PS[:, 0, 0:T], ACT.Exp, scale=-1.0).then_inc(ex_ok, 1)
                    if i % 2 == 0:
                        selT_evac(2 * g + i // 2)
                    act.wait_ge(hd_ps, 4 * g + i + 1)
                    A.activation(hidT, PS[:, 1, T:2 * T].rearrange("p (b n) -> p b n", b=2), ACT.Copy).then_inc(hidT_ok, 1)
                    act.wait_ge(pe_chunk, PE0 + 6 + 24 * g + 6 * i)
                    ydv = yd.rearrange("p (i q n) -> p i q n", i=2, q=2)
                    for q in range(2):
                        A.activation(ydv[64 * (i % 2):64 * (i % 2) + 64, :, q, :], PS[64 * q:64 * q + 64, 4:6, :],
                                     ACT.Copy).then_inc(yd_ok, 1)
            act.wait_ge(routed, 1)
            n_over = act.value_load(ovi[0:1, 0:1], min_val=0, max_val=1)
            with act.If(n_over > 0):
                with act.Fori(0, E) as e:
                    for h in range(H):
                        act.wait_ge(fb_up, 2 * e + h + 1)
                        A.activation(F_ex, PS[:, 0, :], ACT.Exp, scale=-1.0).then_inc(fb_ex, 1)
                        act.wait_ge(fb_tps, 2 * e + h + 1)
                        A.activation(F_hT, PS[:, 2, :], ACT.Copy).then_inc(fb_tok, 1)
            for h in range(H):
                act.wait_ge(f_ss, h + 1)
                A.activation(junk, x1[:, h, :], ACT.Square, accum_out=ssum[:, h:h + 1]).then_inc(f_ms, 1)
                act.wait_ge(f_rt, h + 1)
                A.activation(rstd[:, h:h + 1], rstd[:, h:h + 1], ACT.Sqrt).then_inc(f_r, 1)

        @block.vector
        def _(dve):
            V = nc.vector
            link = chain(dve, v_ch)

            def mean_sq(dst, src, n):
                link(V.tensor_scalar(dst, src, 1.0 / n, EPS, ALU.mult, ALU.add))

            dve.wait_ge(silu_e, 1)
            link(V.tensor_scalar_add(cE, cE, 1.0))
            link(V.reciprocal(cE, cE))
            V.tensor_tensor(cT, cT, cE, ALU.mult).then_inc(silu_c, 1)
            dve.wait_ge(u_ps, 1)
            V.tensor_tensor(u_sb, PS[0:NH, 7, 0:UL], line[:, UL:2 * UL], ALU.add).then_inc(u_ok, 1)
            dve.wait_ge(ss_ok, H)
            V.tensor_scalar(rstd, ssum, 1.0 / D, EPS, ALU.mult, ALU.add).then_inc(ms_ok, 1)
            dve.wait_ge(rt_ok, 1)
            link(V.reciprocal(rstd, rstd))
            dve.wait_ge(cst_in, 16)
            for h in range(H):
                V.tensor_scalar(idr[:, h * P:(h + 1) * P], ident, rstd[:, h:h + 1], None, ALU.mult).then_inc(id_ok, 1)
            for i in range(1, KT // 2, 2):
                dve.wait_ge(tr_ps, i + 1)
                V.tensor_copy(hT[:, 2 * i:2 * i + 2, :], PS[:, i % 4, :].rearrange("p (k t) -> p k t", k=2)).then_inc(tr_dve, 1)

            def mod_row(i):
                dve.wait_ge(brow_in, 16 * (i + 1))
                if i:
                    dve.wait_ge(mod_out, 16 * i)
                V.tensor_tensor(mrow, PS[:, 6, :], brow, ALU.add).then_inc(mod_ok, 1)

            for i in range(2):
                dve.wait_ge(pe_chunk, ADA_CHUNKS * (i + 1))
                mod_row(i)
            dve.wait_ge(mod_in, 32)
            V.scalar_tensor_tensor(A1, A1, 1.0, g1T, ALU.add, ALU.mult).then_inc(ab_ok, 1)
            dve.wait_ge(ab_ok, 1)
            dve.wait_ge(tr_act, KT // 4)
            dve.wait_ge(tr_dve, KT // 4)
            for t in range(1, KT, 2):
                V.tensor_scalar(hT[:, t, :], hT[:, t, :], A1[:, t:t + 1], B1[:, t:t + 1], ALU.mult, ALU.add).then_inc(aff_dve, 1)

            ada_n = [0]

            def ada_chunk(pt_, j):
                w = on_ring(dve, "adv", (pt_, j)).rearrange("p (t n) -> p t n", t=2)
                for r in range(2):
                    t = 2 * j + r
                    if t == 0:
                        if pt_ != G1:
                            dve.wait_ge(mod_ps, MADE.index(pt_) - 2)
                        ins = V.tensor_scalar(ada_acc, w[:, 0, :], cT[:, 0:1], None, ALU.mult)
                    else:
                        dve.wait_ge(accd, ada_n[0])
                        ins = V.scalar_tensor_tensor(ada_acc, w[:, r, :], cT[:, t:t + 1], ada_acc, ALU.mult, ALU.add)
                    ins.then_inc(accd, 1)
                    ada_n[0] += 1

            dve.wait_ge(u_out, 16)
            for i, pt_ in enumerate((G1, SH2, SC2)):
                for j in range(ADA_CHUNKS):
                    ada_chunk(pt_, j)
                dve.wait_ge(mod_ps, i + 1)
                mod_row(2 + i)

            def logits(h):
                dve.wait_ge(s_ps, h + 1)
                if h % 16 == 0:
                    n = number["bias", h // 16]
                    dve.wait_ge(landed[n % RING], 16 * (n // RING + 1))
                if h >= 4:
                    dve.wait_ge(pt_ps, h - 3)
                B = slot(number["bias", h // 16] % RING).rearrange("p (h k) -> p h k", h=16)[:, h % 16, :]
                low = sink[:, h:h + 1] if h < NHA else LOW
                V.tensor_tensor_reduce(out=L[:, h % 4, 0:T], in0=PS[:, h % 2, 0:T], in1=B, scale=1.0, scalar=low,
                                       op0=ALU.add, op1=ALU.max, accum_out=nmx[:, h, 0:1])
                V.tensor_tensor_reduce(out=L[:, h % 4, T:384], in0=PS[:, h % 2, T:384], in1=B[:, P:T], scale=1.0,
                                       scalar=low, op0=ALU.add, op1=ALU.max, accum_out=nmx[:, h, 1:2]).then_inc(lg_ok, 1)
                dve.wait_ge(lg_ok, h + 1)
                V.tensor_scalar(nmx[:, h, :], nmx[:, h, :], -1.0, None, ALU.mult).then_inc(nm_ok, 1)

            def normalise(h):
                dve.wait_ge(p_ok, h + 1)
                if h < NHA:
                    link(V.tensor_tensor(psum_[:, h, :], psum_[:, h, :], esink[:, h, :], ALU.add))
                link(V.reciprocal(rden[:, h, :], psum_[:, h, :]))
                V.tensor_scalar(L[:, h % 4, 0:T], L[:, h % 4, 0:T], rden[:, h, 0:1], None, ALU.mult)
                V.tensor_scalar(L[:, h % 4, T:384], L[:, h % 4, T:384], rden[:, h, 1:2], None, ALU.mult).then_inc(pn_ok, 1)

            def y_evac(b):
                dve.wait_ge(y_ps, b + 1)
                V.tensor_copy(yT[:, b, :], PS[:, 4 + b % 2, 0:T]).then_inc(y_ok, 1)

            for h in range(NH + 3):
                if h < NH:
                    logits(h)
                if 1 <= h <= NH:
                    normalise(h - 1)
                if h >= 3 and h % 2 == 1:
                    y_evac((h - 3) // 2)
            dve.wait_ge(yss_ps, NH // 2)
            for i in range(2):
                ins = V.tensor_scalar(sq[:, i * T:(i + 1) * T], PS[:, 6 + i, 0:T], 1.0 / (NHA * HD), EPS, ALU.mult, ALU.add)
            ins.then_inc(yms_ok, 1)
            dve.wait_ge(yrt_ok, 1)
            link(V.reciprocal(sq[:, :], sq[:, :]))
            dve.wait_ge(y_ok, NH // 2)
            for b in range(KT):
                i = b // (KT // 2)
                V.scalar_tensor_tensor(yT[:, b, :], yT[:, b, :], goT[:, b:b + 1], sq[:, i * T:(i + 1) * T],
                                       ALU.mult, ALU.mult).then_inc(yn_ok, 1)
            gyv = gy[:, :].rearrange("p (h n) -> p h n", h=H)
            for cc in range(WO_CHUNKS):
                dve.wait_ge(pe_chunk, 2 * ADA_CHUNKS + QKV_CHUNKS + cc + 1)
                if cc == 0:
                    dve.wait_ge(xr_ok, 1)
                    dve.wait_ge(mod_in, 16 * 5)
                cols = slice(cc * CW, (cc + 1) * CW)
                gb = g1b[:, cols].unsqueeze(1).to_broadcast([P, H, CW])
                link(V.tensor_tensor(gyv, PS[:, cc % 4, :].rearrange("p (h n) -> p h n", h=H), gb, ALU.mult))
                ins = V.tensor_tensor(x1[:, :, cols], x1[:, :, cols], gyv, ALU.add)
                ins.then_inc(x1_ok, 1)
                ada_chunk(G2, cc)
            dve.wait_ge(x1_ss, WO_CHUNKS)
            link(V.reduce_sum(ssum, part, axis=AX.X))
            V.tensor_scalar(rstd, ssum, 1.0 / D, EPS, ALU.mult, ALU.add).then_inc(ms_ok, 1)
            dve.wait_ge(rt_ok, 2)
            link(V.reciprocal(rstd, rstd))
            for h in range(H):
                V.tensor_scalar(idr[:, h * P:(h + 1) * P], ident, rstd[:, h:h + 1], None, ALU.mult).then_inc(id_ok, 1)
            dve.wait_ge(mod_in, 16 * 5)
            V.scalar_tensor_tensor(A2, A2, 1.0, g2T, ALU.add, ALU.mult).then_inc(ab_ok, 1)
            dve.wait_ge(ab_ok, 2)
            for i in range(1, KT // 2, 2):
                dve.wait_ge(tr_ps, KT // 2 + i + 1)
                for t in (2 * i, 2 * i + 1):
                    last = V.tensor_scalar(h2T[:, t, :], PS[:, i % 4, t % 2 * T:(t % 2 + 1) * T], A2[:, t:t + 1],
                                           B2[:, t:t + 1], ALU.mult, ALU.add)
                last.then_inc(tr_dve, 1)
            dve.wait_ge(mod_ps, 4)
            mod_row(5)
            dve.wait_ge(rw_in, 64)
            dve.wait_ge(rt_ps, 1)
            dve.wait_ge(mod_out, 16 * 6)
            link(V.tensor_tensor(R_lg, PS[:, 5, 0:H * NR].rearrange("p (h n) -> p h n", h=H),
                                 rb.unsqueeze(1).to_broadcast([P, H, NR]), ALU.add))

            def first_largest(dst, val, desc, n, top, tmp):
                link(V.reduce_max(top, val, axis=AX.X))
                link(V.tensor_tensor(tmp, val, top.unsqueeze(2).to_broadcast([P, H, n]), ALU.is_equal))
                link(V.tensor_tensor(tmp, tmp, desc.unsqueeze(1).to_broadcast([P, H, n]), ALU.mult))
                link(V.reduce_max(R_m, tmp, axis=AX.X))
                link(V.tensor_tensor(dst, tmp, R_m.unsqueeze(2).to_broadcast([P, H, n]), ALU.is_equal))

            grp = R_lg[:, :, 0:G]
            first_largest(R_goh, grp, cst[:, C_DG:C_DG + G], G, R_gm, R_t4)
            V.tensor_tensor(R_ge, grp, R_gm.unsqueeze(2).to_broadcast([P, H, G]), ALU.subtract).then_inc(ge_in, 1)
            for h in range(H):
                link(V.tensor_tensor(R_x[:, h], R_lg[:, h, G:NR].rearrange("p (g e) -> p g e", g=G),
                                     R_goh[:, h].unsqueeze(2).to_broadcast([P, G, EPG]), ALU.mult))
                link(V.reduce_sum(R_in[:, h], R_x[:, h].rearrange("p g e -> p e g"), axis=AX.X))
            desc = cst[:, C_DE:C_DE + EPG]
            first_largest(R_o1, R_in, desc, EPG, R_v1, R_t8)
            link(V.scalar_tensor_tensor(R_in2, R_o1, LOW, R_in, ALU.mult, ALU.add))
            first_largest(R_o2, R_in2, desc, EPG, R_v2, R_t8)
            V.tensor_tensor(R_e2, R_v2, R_v1, ALU.subtract).then_inc(e2_in, 1)
            link(V.tensor_tensor(R_t8, R_o1, R_o2, ALU.add))

            def by_group(dst, val):
                for h in range(H):
                    ins = V.tensor_tensor(dst[:, h].rearrange("p (g e) -> p g e", g=G),
                                          R_goh[:, h].unsqueeze(2).to_broadcast([P, G, EPG]),
                                          val[:, h].unsqueeze(1).to_broadcast([P, G, EPG]), ALU.mult)
                return ins
            by_group(R_mem, R_t8).then_inc(mem_ok, 1)
            dve.wait_ge(ge_ok, 1)
            link(V.reduce_sum(R_gm, R_ge, axis=AX.X))
            link(V.reciprocal(R_gm, R_gm))
            dve.wait_ge(e2_ok, 1)
            link(V.tensor_scalar_add(R_w1, R_e2, 1.0))
            link(V.reciprocal(R_w1, R_w1))
            link(V.tensor_tensor(R_w1, R_w1, R_gm, ALU.mult))
            link(V.tensor_tensor(R_e2, R_e2, R_w1, ALU.mult))
            link(V.tensor_tensor(R_o1, R_o1, R_w1.unsqueeze(2).to_broadcast([P, H, EPG]), ALU.mult))
            link(V.tensor_tensor(R_o2, R_o2, R_e2.unsqueeze(2).to_broadcast([P, H, EPG]), ALU.mult))
            link(V.tensor_tensor(R_o1, R_o1, R_o2, ALU.add))
            link(by_group(gates, R_o1))
            dve.wait_ge(pos_ps, 1)
            link(V.scalar_tensor_tensor(posm, PS[:, 7, 0:H * E].rearrange("p (h e) -> p h e", h=H), 1.0, R_mem,
                                        ALU.add, ALU.mult))
            link(V.tensor_scalar(posm, posm, -1.0, None, ALU.add))
            link(V.scalar_tensor_tensor(over, posm, float(SLOTS), gates, ALU.is_ge, ALU.mult))
            link(V.reduce_max(R_m[:, 0:1], PS[:, 7, H * E:(H + 1) * E], axis=AX.X))
            link(V.tensor_scalar(R_m[:, 1:2], R_m[:, 0:1], float(SLOTS), None, ALU.is_gt))
            V.tensor_copy(ovi[:, :], R_m[:, 1:2]).then_inc(routed, 1)
            dve.wait_ge(routed, 1)

            def build_sel(g):
                shape = [P, 4, SLOTS]
                for h in range(H):
                    pos4 = posm[:, h, bass.ds(4 * g, 4)].unsqueeze(2).to_broadcast(shape)
                    V.tensor_tensor(EQ[:, h].rearrange("p (e s) -> p e s", e=4), pos4,
                                    iota.unsqueeze(1).to_broadcast(shape), ALU.is_equal).then_inc(eq_ok, 1)
                dve.wait_ge(eq_ok, 2 * g + 2)
                for h in range(H):
                    gt4 = gates[:, h, bass.ds(4 * g, 4)].unsqueeze(2).to_broadcast(shape)
                    V.tensor_scalar(selr[:, h], EQ[:, h], rstd[:, h:h + 1], None, ALU.mult).then_inc(sel_ok, 1)
                    V.tensor_tensor(selg[:, h].rearrange("p (e s) -> p e s", e=4),
                                    EQ[:, h].rearrange("p (e s) -> p e s", e=4), gt4, ALU.mult).then_inc(sel_ok, 1)

            def acc_add(p):
                for k in range(2 * 4):
                    h, ch = k // 4, k % 4
                    dve.wait_ge(sc_ps, 8 * p + k + 1)
                    a = acc[:, h, 512 * ch:512 * ch + 512]
                    V.tensor_tensor(a, a, PS[:, 6 + k % 2, :], ALU.add).then_inc(acc_ok, 1)

            with dve.Fori(0, E // 4) as g:
                dve.wait_ge(acc_ok, 16 * g + 1)
                build_sel(g)
                for i in range(1, KT // 2, 2):
                    dve.wait_ge(ga_ps, 8 * g + i + 1)
                    for t in (2 * i, 2 * i + 1):
                        last = V.tensor_scalar(hT[:, t, :], PS[:, 3, t % 2 * T:(t % 2 + 1) * T], A2[:, t:t + 1],
                                               B2[:, t:t + 1], ALU.mult, ALU.add)
                    last.then_inc(hg_dve, 1)
                for i in range(4):
                    dve.wait_ge(ex_ok, 4 * g + i + 1)
                    V.tensor_scalar_add(den, ex, 1.0).then_inc(silu_st, 1)
                    dve.wait_ge(silu_st, 12 * g + 3 * i + 1)
                    V.reciprocal(rc, den).then_inc(silu_st, 1)
                    dve.wait_ge(silu_st, 12 * g + 3 * i + 2)
                    V.tensor_tensor(sg, rc, PS[:, 0, 0:T], ALU.mult).then_inc(silu_st, 1)
                    dve.wait_ge(silu_st, 12 * g + 3 * i + 3)
                    V.tensor_tensor(hid, sg, PS[:, 0, T:2 * T], ALU.mult).then_inc(hid_ok, 1)
                    if i == 2:
                        acc_add(2 * g)
                acc_add(2 * g + 1)

            n_over = dve.value_load(ovi[0:1, 0:1], min_val=0, max_val=1)
            with dve.If(n_over > 0):
                for i in range(KT // 2):
                    dve.wait_ge(fb_hps, i + 1)
                    for r in range(2):
                        t = 2 * i + r
                        V.tensor_scalar(F_h[:, t, :], PS[:, 3 + i % 2, r * T:(r + 1) * T], A2[:, t:t + 1],
                                        B2[:, t:t + 1], ALU.mult, ALU.add).then_inc(fb_ht, 1)
                with dve.Fori(0, E) as e:
                    for h in range(H):
                        dve.wait_ge(fb_ex, 2 * e + h + 1)
                        V.tensor_scalar_add(F_ex, F_ex, 1.0).then_inc(fb_link, 1)
                        dve.wait_ge(fb_link, 6 * e + 3 * h + 1)
                        V.reciprocal(F_ex, F_ex).then_inc(fb_link, 1)
                        dve.wait_ge(fb_link, 6 * e + 3 * h + 2)
                        V.tensor_tensor(F_ex, F_ex, PS[:, 0, :], ALU.mult).then_inc(fb_link, 1)
                        dve.wait_ge(fb_link, 6 * e + 3 * h + 3)
                        V.tensor_tensor(F_hid, F_ex, PS[:, 1, :], ALU.mult).then_inc(fb_hid, 1)
                        for ch in range(4):
                            dve.wait_ge(fb_dn, 8 * e + 4 * h + ch + 2)
                            a = acc[:, h, 512 * ch:512 * ch + 512]
                            V.scalar_tensor_tensor(a, PS[:, 3 + ch, :], over[:, h, bass.ds(e, 1)], a,
                                                   ALU.mult, ALU.add).then_inc(fb_acc, 1)
                dve.wait_ge(fb_acc, 8 * E)
            dve.wait_ge(acc_ok, 8 * E // 2 + 1)
            dve.wait_ge(fin_in, 32)
            for h in range(H):
                link(V.tensor_tensor(acc[:, h, :], acc[:, h, :], g2b, ALU.mult))
                V.tensor_tensor(x1[:, h, :], x1[:, h, :], acc[:, h, :], ALU.add).then_inc(f_ss, 1)
            for h in range(H):
                dve.wait_ge(f_ms, h + 1)
                V.tensor_scalar(rstd[:, h:h + 1], ssum[:, h:h + 1], 1.0 / D, EPS, ALU.mult, ALU.add).then_inc(f_rt, 1)
                dve.wait_ge(f_r, h + 1)
                link(V.reciprocal(rstd[:, h:h + 1], rstd[:, h:h + 1]))
                V.scalar_tensor_tensor(x1[:, h, :], x1[:, h, :], rstd[:, h:h + 1], fgb, ALU.mult, ALU.mult).then_inc(o_ok, 1)

        @block.tensor
        def _(pe):
            mm = nc.tensor.matmul
            pe.wait_ge(line_in, 32)
            mm(PS[0:NH, 7, 0:UL], relb, line[:, 0:UL], start=True, stop=True).then_inc(u_ps, 1)

            def transposes(done_act, done_dve):
                for i in range(KT // 2):
                    if i >= 4:
                        pe.wait_ge(tr_act, done_act(i - 4))
                        if done_dve(i - 4):
                            pe.wait_ge(tr_dve, done_dve(i - 4))
                    for r in range(2):
                        for h in range(H):
                            last = mm(PS[:, i % 4, r * T + h * P:r * T + (h + 1) * P],
                                      x1[:, h, 2 * i + r::KT], idr[:, h * P:(h + 1) * P],
                                      start=True, stop=True)
                    last.then_inc(tr_ps, 1)

            pe.wait_ge(id_ok, H)
            pe.wait_ge(x_in, 16)
            transposes(lambda i: (i + 2) // 2, lambda i: (i + 1) // 2)
            pe.wait_ge(silu_c, 1)
            with pe.Fori(0, 2) as i:
                for j in range(ADA_CHUNKS):
                    pe.wait_ge(landed[j], 16 * i + 16)
                    w = slot(j).rearrange("p (t n) -> p t n", t=2)
                    for r in range(2):
                        for q in range(4):
                            last = mm(PS[32 * q:32 * q + 32, 6, :], cT[:, 2 * j + r:2 * j + r + 1].to_broadcast([P, 32]),
                                      w[:, r, 512 * q:512 * q + 512], start=(j + r == 0), stop=(j + r == ADA_CHUNKS))
                    last.then_inc(pe_chunk, 1)
                pe.wait_ge(mod_ok, i + 1)

            def sum_part(i):
                pe.wait_ge(accd, 2 * ADA_CHUNKS * (i + 1))
                pe.wait_ge(mod_ok, 2 + i)
                for q in range(4):
                    last = mm(PS[32 * q:32 * q + 32, 6, :], ones[:, 0:32], ada_acc[:, 512 * q:512 * q + 512],
                              start=True, stop=True)
                last.then_inc(mod_ps, 1)

            n_sum = 0
            for cc in range(QKV_CHUNKS):
                w = on_ring(pe, "qkv", cc).rearrange("p (t n) -> p t n", t=KT)
                if cc >= 4:
                    pe.wait_ge(qkv_ok, cc - 3)
                ps = PS[:, cc % 4, :]
                for sub in range(2):
                    if cc < BV and not (cc == NQ and sub == 1):
                        for t in range(KT):
                            if cc == 0 and sub == 0:
                                pe.wait_ge((aff_act, aff_dve)[t % 2], t // 2 + 1)
                            last = mm(ps[:, sub * T:(sub + 1) * T], w[:, t, sub * P:(sub + 1) * P], hT[:, t, :],
                                      start=(t == 0), stop=(t == KT - 1))
                    elif cc == NQ:
                        for h in range(H):
                            for t in range(KT):
                                last = mm(ps[:, T + h * P:T + (h + 1) * P], hT[:, t, h * P:(h + 1) * P], w[:, t, P:2 * P],
                                          start=(t == 0), stop=(t == KT - 1))
                    else:
                        for t in range(KT):
                            last = mm(ps[:, sub * CW:(sub + 1) * CW], hT[:, t, sub * P:(sub + 1) * P], w[:, t, :],
                                      start=(t == 0), stop=(t == KT - 1))
                last.then_inc(pe_chunk, 1)
                for _ in SUM_AFTER.get(cc, ()):
                    sum_part(n_sum)
                    n_sum += 1

            pe.wait_ge(qkv_ok, QKV_CHUNKS)

            def scores(h):
                if h >= 2:
                    pe.wait_ge(lg_ok, h - 1)
                k = kTa[:, 2 * (h // (NHA // KVA)) + h % 2, :] if h < NHA else kTb[:, h - NHA, :]
                mm(PS[:, h % 2, 0:T], qT[:, h // 2, P:T], k, start=True, stop=True)
                mm(PS[:, h % 2, T:384], qT[:, h // 2, 0:P], k[:, 0:P], start=True, stop=True).then_inc(s_ps, 1)

            def transpose_p(h):
                pe.wait_ge(pn_ok, h + 1)
                if h >= 2:
                    pe.wait_ge(pt_ok, h - 1)
                for k in range(3):
                    last = nc.tensor.transpose(PS[:, 2 + h % 2, k * P:(k + 1) * P], L[:, h % 4, k * P:(k + 1) * P], rev)
                last.then_inc(pt_ps, 1)

            def values(b):
                pe.wait_ge(pt_ok, 2 * b + 2)
                if b >= 2:
                    pe.wait_ge(y_ok, b - 1)
                for (q0, pk, half, st, sp_) in ((P, 0, 0, True, False), (P, 1, 1, False, True), (0, 2, 0, True, True)):
                    for r in range(2):
                        h = 2 * b + r
                        n0 = (h // (NHA // KVA)) * HD if h < NHA else KVA * HD + (h - NHA) * HD
                        last = mm(PS[64 * r:64 * r + 64, 4 + b % 2, q0:q0 + P], v_sb[:, half, n0:n0 + HD],
                                  PT[:, h % 4, pk * P:(pk + 1) * P], start=st, stop=sp_)
                last.then_inc(y_ps, 1)

            def square_sums(b):
                pe.wait_ge(sq_ok, b + 1)
                i, n = divmod(b, KT // 2)
                mm(PS[:, 6 + i, 0:T], ones, sq[:, b % 2 * T:(b % 2 + 1) * T], start=(n == 0),
                   stop=(n == KT // 2 - 1)).then_inc(yss_ps, 1)

            pe.wait_ge(mod_ok, 5)
            for h in range(NH + 3):
                if h < NH:
                    scores(h)
                if 1 <= h <= NH:
                    transpose_p(h - 1)
                if h >= 3 and h % 2 == 1:
                    values((h - 3) // 2)
                if h >= 4 and h % 2 == 0:
                    square_sums((h - 4) // 2)
            for cc in range(WO_CHUNKS):
                w = on_ring(pe, "wo", cc).rearrange("p (t n) -> p t n", t=KT)
                if cc >= 4:
                    pe.wait_ge(x1_ok, cc - 3)
                for h in range(H):
                    for t in range(KT):
                        if cc == 0 and h == 0:
                            pe.wait_ge(yn_ok, t + 1)
                        last = mm(PS[:, cc % 4, h * CW:(h + 1) * CW], yT[:, t, h * P:(h + 1) * P], w[:, t, :],
                                  start=(t == 0), stop=(t == KT - 1))
                last.then_inc(pe_chunk, 1)
            pe.wait_ge(id_ok, 2 * H)
            pe.wait_ge(x1_ok, WO_CHUNKS)
            transposes(lambda i: KT // 4 + (i + 2) // 2, lambda i: KT // 4 + (i + 1) // 2)
            pe.wait_ge(rw_in, 64)
            for t in range(KT):
                pe.wait_ge((tr_act, tr_dve)[t // 2 % 2], KT // 4 + t // 4 + 1)
                last = mm(PS[0:NR, 4, 0:T], wr[:, t, :], h2T[:, t, :], start=(t == 0), stop=(t == KT - 1))
            last.then_inc(rl_ps, 1)
            sum_part(3)
            pe.wait_ge(rl_ok, 1)
            for h in range(H):
                last = mm(PS[:, 5, h * NR:(h + 1) * NR], lgT[:, h * P:(h + 1) * P], ident[0:NR, 0:NR], start=True, stop=True)
            last.then_inc(rt_ps, 1)
            pe.wait_ge(mem_ok, 1)
            mm(PS[:, 7, 0:E], tri, R_mem[:, 0], start=True, stop=True)
            mm(PS[:, 7, E:2 * E], tri, R_mem[:, 1], start=True, stop=False)
            mm(PS[:, 7, E:2 * E], ones, R_mem[:, 0], start=False, stop=True)
            mm(PS[:, 7, 2 * E:3 * E], ones, R_mem[:, 0], start=True, stop=False)
            mm(PS[:, 7, 2 * E:3 * E], ones, R_mem[:, 1], start=False, stop=True).then_inc(pos_ps, 1)

            pe.wait_ge(routed, 1)

            def chunk_at(g, m):
                s = (S0 + m) % RING
                pe.wait_ge(landed[s], 16 * (N0 // RING + 1 + (S0 + m) // RING) + 48 * g)
                return s

            def scatter(p, i0):
                pe.wait_ge(selT_ok, p + 1)
                pe.wait_ge(yd_ok, 4 * p + 4)
                for k in range(8):
                    h, ch = k // 4, k % 4
                    pe.wait_ge(acc_ok, 8 * p + max(1, k))
                    mm(PS[:, 6 + k % 2, :], selT[:, h * P:(h + 1) * P], yd[:, 512 * ch:512 * ch + 512],
                       start=True, stop=True).then_inc(sc_ps, 1)

            def sel_transpose(p, pi):
                for h in range(H):
                    last = nc.tensor.transpose(PS[:, 2, h * P:(h + 1) * P], selg[:, h, pi * P:(pi + 1) * P], ident)
                last.then_inc(st_ps, 1)

            with pe.Fori(0, E // 4) as g:
                pe.wait_ge(sel_ok, 4 * g + 4)
                for i in range(KT // 2):
                    if i >= 2:
                        pe.wait_ge((hg_act, hg_dve)[i % 2], 4 * g + i // 2)
                    for r in range(2):
                        for h in range(H):
                            last = mm(PS[:, 2 + i % 2, r * T:(r + 1) * T], x1[:, h, 2 * i + r::KT], selr[:, h],
                                      start=(h == 0), stop=(h == H - 1))
                    last.then_inc(ga_ps, 1)
                pe.wait_ge(hg_act, 4 * g + 4)
                pe.wait_ge(hg_dve, 4 * g + 4)
                for i in range(4):
                    for half in range(2):
                        s = chunk_at(g, 6 * i + 2 * half)
                        chunk_at(g, 6 * i + 2 * half + 1)
                        w = ring[:, s * SLOT:(s + 2) * SLOT].rearrange("p (m t n) -> p m t n", m=2, n=FE)
                        for t in range(KT // 2):
                            k = half * (KT // 2) + t
                            for j in range(2):
                                last = mm(PS[64 * j:64 * j + 64, 0, :].rearrange("p (m n) -> p m n", m=2),
                                          hT[:, k, i * SLOTS:(i + 1) * SLOTS], w[:, :, t, 256 * j:256 * j + 256],
                                          start=(k == 0), stop=(k == KT - 1))
                        last.then_inc(pe_chunk, 2)
                    if i == 0:
                        sel_transpose(2 * g, 0)
                    if i == 2:
                        scatter(2 * g, 0)
                        sel_transpose(2 * g + 1, 1)
                    pe.wait_ge(hid_ok, 4 * g + i + 1)
                    for b in range(2):
                        last = nc.tensor.transpose(PS[:, 1, T + b * P:T + (b + 1) * P], hid[:, b * P:(b + 1) * P], ident)
                    last.then_inc(hd_ps, 1)
                    pe.wait_ge(hidT_ok, 4 * g + i + 1)
                    if i % 2:
                        pe.wait_ge(yd_ok, 8 * g + 2 * i)
                    for j in range(2):
                        s = chunk_at(g, 6 * i + 4 + j)
                        w = slot(s).rearrange("p (b n) -> p b n", b=2)
                        for b in range(2):
                            for i2 in range(2):
                                for q in range(2):
                                    ch = 2 * i2 + q
                                    last = mm(PS[64 * q:64 * q + 64, 4 + i2, :], hidT[:, b, 64 * j:64 * j + 64],
                                              w[:, b, 512 * ch:512 * ch + 512], start=(j + b == 0), stop=(j + b == 2))
                        last.then_inc(pe_chunk, 1)
                scatter(2 * g + 1, 1)

            n_over = pe.value_load(ovi[0:1, 0:1], min_val=0, max_val=1)
            with pe.If(n_over > 0):
                pe.wait_ge(acc_ok, 8 * E // 2 + 1)
                for i in range(KT // 2):
                    if i >= 2:
                        pe.wait_ge(fb_ht, 2 * (i - 1))
                    for r in range(2):
                        for h in range(H):
                            last = mm(PS[:, 3 + i % 2, r * T + h * P:r * T + (h + 1) * P], x1[:, h, 2 * i + r::KT],
                                      idr[:, h * P:(h + 1) * P], start=True, stop=True)
                    last.then_inc(fb_hps, 1)
                pe.wait_ge(fb_ht, KT)
                pe.sem_inc(fb_dn, 1)
                with pe.Fori(0, E) as e:
                    pe.wait_ge(fb_in, 96 * e + 96)
                    for h in range(H):
                        for m in range(2):
                            for t in range(KT):
                                w = slot(2 * (t // 8) + m).rearrange("p (t n) -> p t n", n=FE)
                                last = mm(PS[:, m, :], F_h[:, t, h * P:(h + 1) * P], w[:, t % 8, :],
                                          start=(t == 0), stop=(t == KT - 1))
                        last.then_inc(fb_up, 1)
                        pe.wait_ge(fb_hid, 2 * e + h + 1)
                        for k in range(4):
                            last = nc.tensor.transpose(PS[:, 2, k * P:(k + 1) * P], F_hid[:, k * P:(k + 1) * P], ident)
                        last.then_inc(fb_tps, 1)
                        pe.wait_ge(fb_tok, 2 * e + h + 1)
                        for ch in range(4):
                            for k in range(4):
                                w = slot(4 + k // 2).rearrange("p (b n) -> p b n", b=2)
                                last = mm(PS[:, 3 + ch, :], F_hT[:, k * P:(k + 1) * P],
                                          w[:, k % 2, 512 * ch:512 * ch + 512], start=(k == 0), stop=(k == 3))
                            last.then_inc(fb_dn, 1)
                        pe.wait_ge(fb_acc, 8 * e + 4 * h + 4)


_INS = ['x', 'c', 'rel_bias', 'w_ada', 'b_ada', 'norm1_g', 'norm2_g', 'w_qkv', 'attn_sinks', 'swa_out_g',
        'moba_out_g', 'w_o', 'w_group', 'b_group', 'w_expert_router', 'b_expert_router', 'w_gate', 'w_up',
        'w_down', 'final_g']


def kernel(**inputs):
    import numpy as _np
    import concourse.bacc as _bacc
    from concourse import mybir as _mybir
    from concourse.bass_utils import run_bass_kernel_spmd as _run

    nc = _bacc.Bacc("TRN2", target_bir_lowering=False, num_devices=1, dynamic_dma_scratch_size=8192)
    table, lines = constants()
    arrays, args = {}, []
    for name in _INS:
        arrays[f"in_{name}"] = _np.ascontiguousarray(inputs[name])
    arrays["const_table"], arrays["const_lines"] = table, lines
    for name, a in arrays.items():
        args.append(nc.dram_tensor(name, a.shape, _mybir.dt.from_np(a.dtype), kind="ExternalInput").ap())
    shape = arrays["in_x"].shape
    args.append(nc.dram_tensor("out_0", shape, _mybir.dt.float32, kind="ExternalOutput").ap())
    layer_kernel(nc, *args)
    r = _run(nc, [arrays], core_ids=[0])
    return r.results[0]["out_0"]
```

```python
import math
from contextlib import ExitStack

import numpy as np
import concourse.bass as bass
from concourse import mybir

F32 = mybir.dt.float32
I32 = mybir.dt.int32
ALU = mybir.AluOpType
ACT = mybir.ActivationFunctionType
AX = mybir.AxisListType

P = 128
D = 2048
T = 256
H = T // P
KT = D // P
HD = 64
NHA, NHB = 16, 16
NH = NHA + NHB
KVA = 2
WINDOW = 128
BUCKETS = 32
MAX_DIST = 2048
G, EPG = 4, 8
E = G * EPG
FE = 512
NR = G + E
SLOTS = 64
EPS = 1e-6
NEG = -1e30
LOW = -3.0e38
SCALE = 1.0 / math.sqrt(HD)

RING = 8
SLOT = 4096
CW = 256
QKV_CHUNKS = (NHA * HD + 2 * KVA * HD + 3 * NHB * HD) // CW
WO_CHUNKS = D // CW
ADA_CHUNKS = KT // 2
SH1, SC1, G1, SH2, SC2, G2 = range(6)
UL = 384
EXP_CHUNKS = 6


def rel_bucket(dist):
    n = np.maximum(dist, 0)
    exact = BUCKETS // 2
    nf = np.maximum(n, 1).astype(np.float32)
    large = exact + (np.log(nf / np.float32(exact)) / np.float32(math.log(MAX_DIST / exact))
                     * np.float32(BUCKETS - exact)).astype(np.int32)
    return np.where(n < exact, n, np.minimum(large, BUCKETS - 1))


GROUP = ([(0, k) for k in range(4)] + [(1, k) for k in range(4)] + [(0, 4), (0, 5)] + [(2, k) for k in range(4)]
         + [(1, 4), (1, 5)] + [(3, k) for k in range(4)] + [(2, 4), (2, 5), (3, 4), (3, 5)])
GU_AT = [GROUP.index((i, 0)) for i in range(4)]
DN_AT = [GROUP.index((i, 4)) for i in range(4)]
GU_END = [k + 4 for k in GU_AT]
DN_END = [k + 2 for k in DN_AT]

C_ID, C_TRI, C_ONE = 0, P, 2 * P
C_IOTA = 3 * P
C_DG = C_IOTA + SLOTS
C_DE = C_DG + G
C_REV = C_DE + EPG
C_N = C_REV + P


def constants():
    c = np.zeros((P, C_N), np.float32)
    c[:, C_ID:C_ID + P] = np.eye(P)
    c[:, C_TRI:C_TRI + P] = np.triu(np.ones((P, P)), 1)
    c[:, C_ONE:C_ONE + P] = 1.0
    c[:, C_IOTA:C_IOTA + SLOTS] = np.arange(SLOTS)
    c[:, C_DG:C_DG + G] = np.arange(G, 0, -1)
    c[:, C_DE:C_DE + EPG] = np.arange(EPG, 0, -1)
    c[:, C_REV:C_REV + P] = np.eye(P)[::-1]
    dist = 255 - np.arange(UL)
    line = np.zeros((BUCKETS, 2 * UL), np.float32)
    line[rel_bucket(dist), np.arange(UL)] = (dist >= 0)
    bad = np.zeros((NH, UL), np.float32)
    bad[:NHA, (dist < 0) | (dist >= WINDOW)] = NEG
    bad[NHA:, dist < 0] = NEG
    line[:, UL:] = bad
    return c, line


def stream_plan():
    order = [("ada", (part, j), "pe") for part in (SH1, SC1) for j in range(ADA_CHUNKS)]
    vec = [("adv", (part, j), "dve") for part in (G1, SH2, SC2) for j in range(ADA_CHUNKS)]
    done = 0
    for c in range(QKV_CHUNKS):
        order.append(("qkv", c, "pe"))
        upto = min(len(vec), (c + 1) * len(vec) // (QKV_CHUNKS - 2))
        order += vec[done:upto]
        done = upto
    order += [("bias", 0, "bias"), ("bias", 1, "bias"), ("x", 0, "x")]
    for c in range(WO_CHUNKS):
        order += [("wo", c, "pe"), ("adv", (G2, c), "dve")]
    number = {(k, i): n for n, (k, i, _) in enumerate(order)}
    seen, free = {}, []
    for _, _, who in order:
        seen[who] = seen.get(who, 0) + 1
        free.append((who, seen[who]))
    return order, number, free


def layer_kernel(nc, x, c, rel_bias, w_ada, b_ada, norm1_g, norm2_g, w_qkv, attn_sinks, swa_out_g,
                 moba_out_g, w_o, w_group, b_group, w_router, b_router, w_gate, w_up, w_down,
                 final_g, cst_d, line_d, out):
    order, number, free_at = stream_plan()
    N0 = len(order)
    PE0 = sum(who == "pe" for _, _, who in order)
    assert N0 % 2 == 0
    S0 = N0 % RING

    x_v = x[0].rearrange("(h p) n -> p h n", p=P)
    out_v = out[0].rearrange("(h p) n -> p h n", p=P)
    ada_v = w_ada[0].rearrange("(p t) n -> p t n", t=KT)
    qkv_v = w_qkv[0].rearrange("(t p) n -> p t n", p=P)
    wo_v = w_o[0].rearrange("(t p) n -> p t n", p=P)
    gate_v = w_gate[0].rearrange("e (p t) n -> e p t n", t=KT)
    up_v = w_up[0].rearrange("e (p t) n -> e p t n", t=KT)
    down_v = w_down[0].rearrange("e (k p) n -> e p k n", p=P)
    u_scr = nc.dram_tensor("u_scr", [NH, UL], F32, kind="Internal").ap()
    m_scr = nc.dram_tensor("m_scr", [6, D], F32, kind="Internal").ap()

    with ExitStack() as ctx:
        def sb(name, n, dt=F32):
            return ctx.enter_context(nc.sbuf_tensor(name, [P, n], dt))

        def sem(name):
            return ctx.enter_context(nc.semaphore(name))

        ring = sb("ring", RING * SLOT)
        r1 = sb("r1", H * D)
        r2 = sb("r2", H * D)
        r3 = sb("r3", H * D)
        W = sb("W", 7424)
        cst = sb("cst", C_N)
        vrow = sb("vrow", P)
        gy = sb("gy", H * CW)
        idr = sb("idr", H * P)
        sq = sb("sq", 2 * T)
        sm = sb("sm", 640)
        ovi = sb("ovi", 1, I32)
        PS = ctx.enter_context(nc.psum_tensor("PS", [P, 8, 512], F32))

        def slot(s):
            return ring[:, s * SLOT:(s + 1) * SLOT]

        x1 = r1[:, :].rearrange("p (h n) -> p h n", h=H)
        qT = r1[:, :].rearrange("p (b t) -> p b t", t=T)
        hT = r2[:, :].rearrange("p (k t) -> p k t", t=T)
        yT = hT
        kTb = r3[:, :].rearrange("p (b t) -> p b t", t=T)
        h2T = kTb
        acc = r3[:, :].rearrange("p (h n) -> p h n", h=H)
        fgb = r2[:, 0:D]
        VW = (KVA + NHB) * HD
        v_sb = W[:, 0:H * VW].rearrange("p (h n) -> p h n", h=H)
        o = H * VW
        kTa = W[:, o:o + 2 * KVA * T].rearrange("p (b t) -> p b t", t=T)
        o += 2 * KVA * T
        L = W[:, o:o + 4 * 384].rearrange("p (b t) -> p b t", b=4)
        PT = W[:, o + 4 * 384:o + 8 * 384].rearrange("p (b t) -> p b t", b=4)
        ada_acc = W[:, o:o + D]
        mrow = W[:, o + D:o + D + 512]
        brow = W[:, o + D + 512:o + D + 1024]
        line = W[0:NH, o:o + 2 * UL]
        relb = W[0:BUCKETS, o + 2 * UL:o + 2 * UL + NH]
        u_sb = W[0:NH, o + 2 * UL + NH:o + 3 * UL + NH]
        g1b = W[:, 0:D]
        wr = W[:, o - 4 * T:o - 4 * T + KT * NR].rearrange("p (t n) -> p t n", n=NR)
        lgT = W[0:NR, o - 4 * T + KT * NR:o - 4 * T + KT * NR + T]
        RT0 = o
        yd = W[:, 0:D]
        EQ = W[:, 2048:2560].rearrange("p (h n) -> p h n", h=H)
        selr = W[:, 2560:3072].rearrange("p (h n) -> p h n", h=H)
        selg = W[:, 3072:3584].rearrange("p (h n) -> p h n", h=H)
        selT = W[:, 3584:3840]
        ex, den, rc, sg, hid = [W[:, 3840 + T * i:3840 + T * (i + 1)] for i in range(5)]
        hidT = W[:, 5120:5376].rearrange("p (b n) -> p b n", b=2)
        g2b = W[:, 5376:5376 + D]
        junk = W[:, 0:D]

        ident = cst[:, C_ID:C_ID + P]
        rev = cst[:, C_REV:C_REV + P]
        tri = cst[:, C_TRI:C_TRI + P]
        ones = cst[:, C_ONE:C_ONE + P]
        iota = cst[:, C_IOTA:C_IOTA + SLOTS]

        at = [0]

        def small(n):
            at[0] += n
            assert at[0] <= 640
            return sm[:, at[0] - n:at[0]]

        ssum, rstd = small(H), small(H)
        cT, cE = small(KT), small(KT)
        g1T, goT, g2T = small(KT), small(KT), small(KT)
        g1goT = sm[:, at[0] - 3 * KT:at[0] - KT]
        A1, B1, A2, B2 = small(KT), small(KT), small(KT), small(KT)
        sink = small(NHA)
        nmx, psum_, rden = (small(NH * 2).rearrange("p (h t) -> p h t", t=2) for _ in range(3))
        esink = small(NHA * 2).rearrange("p (h t) -> p h t", t=2)
        part = small(H * WO_CHUNKS).rearrange("p (h c) -> p h c", h=H)
        over = small(H * E).rearrange("p (h e) -> p h e", h=H)
        posx, gatex = (small(H * (E + 4)).rearrange("p (h e) -> p h e", h=H) for _ in range(2))
        posm, gates = posx[:, :, 0:E], gatex[:, :, 0:E]
        rb = W[:, RT0 - 4 * T + KT * NR + T:RT0 - 4 * T + KT * NR + T + NR]
        assert KT * NR + T + NR <= 4 * T
        rt_at = [RT0]

        def rt(*dims):
            n = int(np.prod(dims))
            v = W[:, rt_at[0]:rt_at[0] + n]
            rt_at[0] += n
            names = "abc"[:len(dims)]
            if len(dims) == 1:
                return v
            spec = "p (" + " ".join(names) + ") -> p " + " ".join(names)
            return v.rearrange(spec, **dict(zip(names, dims)))

        R_lg, R_goh, R_t4, R_ge, R_x = rt(H, NR), rt(H, G), rt(H, G), rt(H, G), rt(H, G, EPG)
        R_in, R_in2, R_o1, R_o2, R_t8 = (rt(H, EPG) for _ in range(5))
        R_gm, R_v1, R_v2, R_m, R_e2, R_w1 = (rt(H) for _ in range(6))
        R_mem = rt(H, E)
        F_h = slot(6).rearrange("p (k t) -> p k t", t=T)
        F_ex, F_hid, F_hT, F_y = (slot(7)[:, i * FE:(i + 1) * FE] for i in range(4))

        x_in, cst_in, small_in, line_in = sem("x_in"), sem("cst_in"), sem("small_in"), sem("line_in")
        c_in, brow1_in, vrow_in, vec_ps, mc_ps, mc_ok = (sem(n) for n in ("c_in", "brow1_in", "vrow_in", "vec_ps", "mc_ps", "mc_ok"))
        landed = [sem(f"landed{s}") for s in range(RING)]
        pe_chunk = sem("pe_chunk")
        ab_ok = sem("ab_ok")
        brow_in = sem("brow_in")
        kz = sem("kz")
        u_ps, u_ok, u_out = sem("u_ps"), sem("u_ok"), sem("u_out")
        ss_ok, ms_ok, rt_ok, id_ok = sem("ss_ok"), sem("ms_ok"), sem("rt_ok"), sem("id_ok")
        tr_ps, tr_act, tr_dve = sem("tr_ps"), sem("tr_act"), sem("tr_dve")
        aff_act, aff_dve = sem("aff_act"), sem("aff_dve")
        silu_e, silu_c = sem("silu_e"), sem("silu_c")
        accd, mod_ps, mod_ok, mod_out, mod_in = sem("accd"), sem("mod_ps"), sem("mod_ok"), sem("mod_out"), sem("mod_in")
        qkv_ok = sem("qkv_ok")
        s_ps, lg_ok, nm_ok, p_ok, sum_ok = sem("s_ps"), sem("lg_ok"), sem("nm_ok"), sem("p_ok"), sem("sum_ok")
        pn_ok, pt_ps, pt_ok, y_ps, y_ok, sq_ok, yss_ps = (sem("pn_ok"), sem("pt_ps"), sem("pt_ok"), sem("y_ps"),
                                                          sem("y_ok"), sem("sq_ok"), sem("yss_ps"))
        yms_ok, yrt_ok, yn_ok = sem("yms_ok"), sem("yrt_ok"), sem("yn_ok")
        x1_ok, x1_ss, xr_ok = sem("x1_ok"), sem("x1_ss"), sem("xr_ok")
        rw_in = sem("rw_in")
        rl_ps, rl_ok, rt_ps, pos_ps, mem_ok, ge_in, ge_ok, e2_in, e2_ok = (
            sem("rl_ps"), sem("rl_ok"), sem("rt_ps"), sem("pos_ps"), sem("mem_ok"), sem("ge_in"),
            sem("ge_ok"), sem("e2_in"), sem("e2_ok"))
        routed = sem("routed")
        eq_ok, sel_ok = sem("eq_ok"), sem("sel_ok")
        ga_ps, hg_act, hg_dve = sem("ga_ps"), sem("hg_act"), sem("hg_dve")
        ex_ok, silu_st, hid_ok, hd_ps, hidT_ok = sem("ex_ok"), sem("silu_st"), sem("hid_ok"), sem("hd_ps"), sem("hidT_ok")
        st_ps, selT_ok, yd_ok, sc_ps, acc_ok = sem("st_ps"), sem("selT_ok"), sem("yd_ok"), sem("sc_ps"), sem("acc_ok")
        fb_in, fb_up, fb_ex, fb_hid, fb_tps, fb_tok, fb_dn, fb_acc, fb_ht, fb_hps, fb_link = (
            [sem(f"fb{i}") for i in range(11)])
        fb_y = sem("fb_y")
        fg_in = sem("fg_in")
        fin_in, f_ss, f_ms, f_rt, f_r, o_ok, o_out = (sem("fin_in"), sem("f_ss"), sem("f_ms"), sem("f_rt"),
                                                    sem("f_r"), sem("o_ok"), sem("o_out"))
        v_ch, a_ch = sem("v_ch"), sem("a_ch")

        def on_ring(eng, kind, i):
            n = number[kind, i]
            eng.wait_ge(landed[n % RING], 16 * (n // RING + 1))
            return slot(n % RING)

        def chain(eng, s):
            n = [0]

            def link(ins):
                n[0] += 1
                ins.then_inc(s, 1)
                eng.wait_ge(s, n[0])
            return link

        MADE = [SH1, SC1, G1, SH2, SC2, G2]
        SUM_AFTER = {}
        for i, pt_ in enumerate((G1, SH2, SC2)):
            n = number["adv", (pt_, ADA_CHUNKS - 1)]
            SUM_AFTER.setdefault(min([q for q in range(QKV_CHUNKS) if number["qkv", q] > n],
                                     default=QKV_CHUNKS - 1), []).append(pt_)
        NQ = NHA * HD // CW
        BQ, BK, BV = NQ + 1, NQ + 1 + NHB * HD // CW, NQ + 1 + 2 * NHB * HD // CW
        CPB = CW // P

        block = ctx.enter_context(nc.Block())

        def quadrant_rows(pt_):
            return bass.AP(b_ada.tensor, b_ada.offset + pt_ * D, [[512, 4], [0, 32], [1, 512]])

        @block.sync
        def _(sp):
            sp.dma_start(cT, c[0].rearrange("(p t) -> p t", t=KT)).then_inc(c_in, 16)
            sp.dma_start(cst[:, :], cst_d).then_inc(cst_in, 16)
            for pt_, dst in ((SH1, brow), (SC1, sq[:, :])):
                sp.dma_start(dst, quadrant_rows(pt_)).then_inc(brow1_in, 16)
            sp.dma_start(vrow[0:KT, :], norm1_g[0].rearrange("(t p) -> t p", p=P)).then_inc(vrow_in, 16)
            for i, v in enumerate((swa_out_g, moba_out_g)):
                sp.dma_start(vrow[KT + i * KT // 2:KT + (i + 1) * KT // 2, :],
                             v[0].rearrange("(t p) -> t p", p=P)).then_inc(vrow_in, 16)
            sp.dma_start(x1, x_v).then_inc(x_in, 16)

            def read_by(sp, who, count):
                s, each = {"pe": (pe_chunk, 1), "dve": (accd, 2), "bias": (lg_ok, NH // 2), "x": (xr_ok, 1)}[who]
                sp.wait_ge(s, each * count)

            def load(n, dst, src):
                if n >= RING:
                    who, count = free_at[n - RING]
                    read_by(sp, who, count)
                sp.dma_start(dst, src).then_inc(landed[n % RING], 16)

            for n, (kind, i, _) in enumerate(order):
                s = slot(n % RING)
                if kind in ("ada", "adv"):
                    src = ada_v[:, 2 * i[1]:2 * i[1] + 2, i[0] * D:(i[0] + 1) * D]
                    load(n, s.rearrange("p (t n) -> p t n", t=2), src)
                elif kind == "qkv":
                    load(n, s.rearrange("p (t n) -> p t n", t=KT), qkv_v[:, :, i * CW:(i + 1) * CW])
                elif kind == "bias":
                    if i == 0:
                        sp.wait_ge(u_out, 16)
                    src = bass.AP(u_scr.tensor, u_scr.offset + i * 16 * UL, [[1, P], [UL, 16], [1, T]])
                    load(n, s.rearrange("p (h k) -> p h k", h=16), src)
                elif kind == "x":
                    load(n, s.rearrange("p (h n) -> p h n", h=H), x_v)
                else:
                    load(n, s.rearrange("p (t n) -> p t n", t=KT), wo_v[:, :, i * CW:(i + 1) * CW])

            def expert_chunk(e, k, s):
                if k < 4:
                    v = (gate_v, up_v)[k % 2]
                    t0 = (k // 2) * (KT // 2)
                    return (slot(s).rearrange("p (t n) -> p t n", n=FE), v[e, :, t0:t0 + KT // 2, :])
                return (slot(s).rearrange("p (t n) -> p t n", n=D), down_v[e, :, 2 * (k - 4):2 * (k - 4) + 2, :])

            for m in range(EXP_CHUNKS * E):
                if m < RING:
                    read_by(sp, *free_at[N0 + m - RING])
                else:
                    sp.wait_ge(pe_chunk, PE0 + m - RING + 1)
                i, k = GROUP[m % 24]
                dst, src = expert_chunk(4 * (m // 24) + i, k, (S0 + m) % RING)
                sp.dma_start(dst, src).then_inc(landed[(S0 + m) % RING], 16)

            sp.wait_ge(pe_chunk, PE0 + EXP_CHUNKS * E)
            sp.wait_ge(routed, 1)
            n_over = sp.value_load(ovi[0:1, 0:1], min_val=0, max_val=1)
            with sp.If(n_over > 0):
                with sp.Fori(0, E) as e:
                    sp.wait_ge(fb_dn, 8 * e + 1)
                    for k in range(4):
                        v = (gate_v, up_v)[k % 2]
                        t0 = (k // 2) * (KT // 2)
                        sp.dma_start(slot(k).rearrange("p (t n) -> p t n", n=FE),
                                     v[e, :, t0:t0 + KT // 2, :]).then_inc(fb_in, 16)
                    for k in range(2):
                        sp.dma_start(slot(4 + k).rearrange("p (t n) -> p t n", n=D),
                                     down_v[e, :, 2 * k:2 * k + 2, :]).then_inc(fb_in, 16)
            for k in range(2 * H):
                h, n0 = k // 2, k % 2 * (D // 2)
                sp.wait_ge(o_ok, k + 1)
                sp.dma_start(out_v[:, h, n0:n0 + D // 2], acc[:, h, n0:n0 + D // 2]).then_inc(o_out, 16)
            sp.wait_ge(o_out, 16 * 2 * H)

        @block.gpsimd
        def _(pool):
            pool.dma_start(line, line_d).then_inc(line_in, 16)
            pool.dma_start(relb, rel_bias).then_inc(line_in, 16)
            pool.dma_start(g2T, norm2_g[0].rearrange("(p t) -> p t", t=KT)).then_inc(small_in, 16)
            pool.dma_start(sink, bass.AP(attn_sinks.tensor, attn_sinks.offset, [[0, P], [1, NHA]])).then_inc(small_in, 16)
            nc.gpsimd.memset(r3[:, :], 0.0).then_inc(kz, 1)
            nc.gpsimd.memset(W[:, H * VW:H * VW + 2 * KVA * T], 0.0).then_inc(kz, 1)
            pool.wait_ge(u_ok, 1)
            pool.dma_start(u_scr, u_sb).then_inc(u_out, 16)
            for i, pt_ in enumerate(MADE[2:]):
                pool.wait_ge(mod_ok, i + 2 if i else 1)
                if pt_ == G2:
                    pool.wait_ge(y_ok, NH // 2)
                    pool.dma_start(g1b, bass.AP(m_scr.tensor, m_scr.offset + G1 * D, [[0, P], [1, D]])).then_inc(mod_in, 16)
                    pool.dma_start(wr[:, :, 0:G], w_group[0].rearrange("(p t) n -> p t n", t=KT)).then_inc(rw_in, 16)
                    pool.dma_start(wr[:, :, G:NR], w_router[0].rearrange("(p t) n -> p t n", t=KT)).then_inc(rw_in, 16)
                    pool.dma_start(rb[:, 0:G], bass.AP(b_group.tensor, b_group.offset, [[0, P], [1, G]])).then_inc(rw_in, 16)
                    pool.dma_start(rb[:, G:NR], bass.AP(b_router.tensor, b_router.offset, [[0, P], [1, E]])).then_inc(rw_in, 16)
                pool.dma_start(brow, quadrant_rows(pt_)).then_inc(brow_in, 16)
                pool.wait_ge(mod_ok, i + 3)
                rows = bass.AP(mrow.tensor, mrow.offset, [[mrow.ap[0][0] * 32, 4], [1, 512]])
                pool.dma_start(m_scr[pt_].rearrange("(q n) -> q n", q=4), rows).then_inc(mod_out, 16)
                pool.wait_ge(mod_out, 16 * (i + 1))
                if pt_ not in (G1, G2):
                    dst = {SH2: B2, SC2: A2}[pt_]
                    pool.dma_start(dst, m_scr[pt_].rearrange("(p t) -> p t", t=KT)).then_inc(mod_in, 16)
            pool.wait_ge(rl_ps, 1)
            nc.gpsimd.tensor_copy(r3[:, :], r1[:, :]).then_inc(acc_ok, 1)
            pool.dma_start(g2b, bass.AP(m_scr.tensor, m_scr.offset + G2 * D, [[0, P], [1, D]])).then_inc(fin_in, 16)
            pool.wait_ge(pe_chunk, PE0 + 24 * (E // 4 - 1) + GU_END[3])
            pool.dma_start(fgb, bass.AP(final_g.tensor, final_g.offset, [[0, P], [1, D]])).then_inc(fg_in, 16)

        @block.scalar
        def _(act):
            A = nc.scalar
            act.wait_ge(c_in, 16)
            A.activation(cE, cT, ACT.Exp, scale=-1.0).then_inc(silu_e, 1)
            act.wait_ge(x_in, 16)
            for h in range(H):
                if h:
                    act.wait_ge(ss_ok, h)
                A.activation(junk, x1[:, h, :], ACT.Square, accum_out=ssum[:, h:h + 1]).then_inc(ss_ok, 1)
            act.wait_ge(ms_ok, 1)
            A.activation(rstd, rstd, ACT.Sqrt).then_inc(rt_ok, 1)
            for i in range(0, KT // 2, 2):
                act.wait_ge(tr_ps, i + 1)
                A.activation(hT[:, 2 * i:2 * i + 2, :], PS[:, i % 4, :].rearrange("p (k t) -> p k t", k=2),
                             ACT.Copy).then_inc(tr_act, 1)
            act.wait_ge(ab_ok, 1)
            act.wait_ge(tr_act, KT // 4)
            act.wait_ge(tr_dve, KT // 4)
            for t in range(0, KT, 2):
                A.activation(hT[:, t, :], hT[:, t, :], ACT.Identity, scale=A1[:, t:t + 1],
                             bias=B1[:, t:t + 1]).then_inc(aff_act, 1)
            for cc in range(QKV_CHUNKS):
                act.wait_ge(pe_chunk, 2 * ADA_CHUNKS + cc + 1)
                ps = PS[:, cc % 4, :]
                ps2 = ps.rearrange("p (b t) -> p b t", b=2)
                if cc < NQ or BQ <= cc < BK:
                    b0 = cc * CPB if cc < NQ else NHA // 2 + (cc - BQ) * CPB
                    back = bass.AP(ps.tensor, ps.offset + P - 1, [list(ps.ap[0]), [P, 2 * CPB], [-1, P]])
                    A.activation(qT[:, b0:b0 + CPB, :].rearrange("p b (h t) -> p (b h) t", h=H), back, ACT.Copy,
                                 scale=SCALE).then_inc(qkv_ok, 1)
                elif cc == NQ:
                    act.wait_ge(kz, 2)
                    for g in range(KVA):
                        for r in range(2):
                            A.activation(kTa[64 * r:64 * r + 64, 2 * g + r, :], ps[64 * g:64 * g + 64, 0:T], ACT.Copy)
                    A.activation(v_sb[:, :, 0:P], ps[:, T:2 * T].rearrange("p (h n) -> p h n", h=H),
                                 ACT.Copy).then_inc(qkv_ok, 1)
                elif cc < BV:
                    b0 = (cc - BK) * CPB
                    for r in range(2):
                        dst = kTb[64 * r:64 * r + 64, 2 * b0 + r:2 * b0 + r + 3:2, :]
                        last = A.activation(dst, ps2[64 * r:64 * r + 64], ACT.Copy)
                    last.then_inc(qkv_ok, 1)
                else:
                    n0 = P + (cc - BV) * CW
                    A.activation(v_sb[:, :, n0:n0 + CW], ps2, ACT.Copy).then_inc(qkv_ok, 1)

            def exps(h):
                act.wait_ge(nm_ok, h + 1)
                A.activation(L[:, h % 4, 0:T], L[:, h % 4, 0:T], ACT.Exp, bias=nmx[:, h, 0:1],
                             accum_out=psum_[:, h, 0:1])
                last = A.activation(L[:, h % 4, T:384], L[:, h % 4, T:384], ACT.Exp, bias=nmx[:, h, 1:2],
                                    accum_out=psum_[:, h, 1:2])
                if h < NHA:
                    last = A.activation(esink[:, h, :], nmx[:, h, :], ACT.Exp, bias=sink[:, h:h + 1])
                last.then_inc(p_ok, 1)

            def pt_evac(h):
                act.wait_ge(pt_ps, h + 1)
                if h >= 4:
                    act.wait_ge(y_ps, (h - 4) // 2 + 1)
                A.activation(PT[:, h % 4, :], PS[:, 2 + h % 2, 0:384], ACT.Copy).then_inc(pt_ok, 1)

            def squares(b):
                act.wait_ge(y_ok, b + 1)
                if b >= 2:
                    act.wait_ge(yss_ps, b - 1)
                A.activation(sq[:, b % 2 * T:(b % 2 + 1) * T], yT[:, b, :], ACT.Square).then_inc(sq_ok, 1)

            act.wait_ge(mod_out, 16 * 3)
            act.wait_ge(small_in, 32)
            for h in range(NH + 4):
                if h < NH:
                    exps(h)
                if 2 <= h < NH + 2:
                    pt_evac(h - 2)
                if h >= 5 and h % 2 == 1:
                    squares((h - 5) // 2)
            act.wait_ge(yms_ok, 1)
            A.activation(sq[:, :], sq[:, :], ACT.Sqrt).then_inc(yrt_ok, 1)
            act.wait_ge(s_ps, NH)
            xs = on_ring(act, "x", 0)
            A.activation(r1[:, :], xs, ACT.Copy).then_inc(xr_ok, 1)
            for cc in range(WO_CHUNKS):
                act.wait_ge(x1_ok, cc + 1)
                for h in range(H):
                    last = A.activation(sq[:, h * CW:(h + 1) * CW], x1[:, h, cc * CW:(cc + 1) * CW],
                                        ACT.Square, accum_out=part[:, h, cc:cc + 1])
                last.then_inc(x1_ss, 1)
                if cc < WO_CHUNKS - 1:
                    act.wait_ge(x1_ss, cc + 1)
            act.wait_ge(ms_ok, 2)
            A.activation(rstd, rstd, ACT.Sqrt).then_inc(rt_ok, 1)
            act.wait_ge(ab_ok, 2)
            for i in range(0, KT // 2, 2):
                act.wait_ge(tr_ps, KT // 2 + i + 1)
                for r in range(2):
                    t = 2 * i + r
                    last = A.activation(h2T[:, t, :], PS[:, i % 4, r * T:(r + 1) * T], ACT.Identity,
                                        scale=A2[:, t:t + 1], bias=B2[:, t:t + 1])
                last.then_inc(tr_act, 1)
            act.wait_ge(rl_ps, 1)
            A.activation(lgT, PS[0:NR, 4, 0:T], ACT.Copy).then_inc(rl_ok, 1)
            act.wait_ge(ge_in, 1)
            A.activation(R_ge, R_ge, ACT.Exp).then_inc(ge_ok, 1)
            act.wait_ge(e2_in, 1)
            A.activation(R_e2, R_e2, ACT.Exp).then_inc(e2_ok, 1)

            def hg_evac(g):
                for i in range(0, KT // 2, 2):
                    act.wait_ge(ga_ps, 8 * g + i + 1)
                    for t in (2 * i, 2 * i + 1):
                        last = A.activation(hT[:, t, :], PS[:, 2, t % 2 * T:(t % 2 + 1) * T], ACT.Identity,
                                            scale=A2[:, t:t + 1], bias=B2[:, t:t + 1])
                    last.then_inc(hg_act, 1)

            def selT_evac(p):
                act.wait_ge(st_ps, p + 1)
                A.activation(selT, PS[:, 2, 0:T], ACT.Copy).then_inc(selT_ok, 1)

            with act.Fori(0, E // 4) as g:
                hg_evac(g)

                def exp_gate(i):
                    act.wait_ge(pe_chunk, PE0 + 24 * g + GU_END[i])
                    if i:
                        act.wait_ge(hid_ok, 4 * g + i)
                    A.activation(ex, PS[:, i % 2, 0:T], ACT.Exp, scale=-1.0).then_inc(ex_ok, 1)

                def hidT_evac(i):
                    act.wait_ge(hd_ps, 4 * g + i + 1)
                    A.activation(hidT, PS[:, 3, 0:T].rearrange("p (b n) -> p b n", b=2), ACT.Copy).then_inc(hidT_ok, 1)

                exp_gate(0)
                selT_evac(2 * g)
                exp_gate(1)
                hidT_evac(0)
                exp_gate(2)
                hidT_evac(1)
                exp_gate(3)
                hidT_evac(2)
                selT_evac(2 * g + 1)
                hidT_evac(3)
            act.wait_ge(routed, 1)
            n_over = act.value_load(ovi[0:1, 0:1], min_val=0, max_val=1)
            with act.If(n_over > 0):
                with act.Fori(0, E) as e:
                    for h in range(H):
                        act.wait_ge(fb_up, 2 * e + h + 1)
                        A.activation(F_ex, PS[:, 0, :], ACT.Exp, scale=-1.0).then_inc(fb_ex, 1)
                        act.wait_ge(fb_tps, 2 * e + h + 1)
                        A.activation(F_hT, PS[:, 2, :], ACT.Copy).then_inc(fb_tok, 1)
                act.wait_ge(fb_acc, 8 * E)
            for h in range(H):
                for ch in range(4):
                    act.wait_ge(acc_ok, 8 * (E // 2 - 1) + 4 * h + ch + 2)
                    A.activation(F_ex, acc[:, h, 512 * ch:512 * ch + 512], ACT.Square,
                                 accum_out=part[:, h, ch:ch + 1]).then_inc(f_ms, 1)
                    act.wait_ge(f_ms, 4 * h + ch + 1)
                act.wait_ge(f_rt, h + 1)
                A.activation(rstd[:, h:h + 1], rstd[:, h:h + 1], ACT.Sqrt).then_inc(f_r, 1)

        @block.vector
        def _(dve):
            V = nc.vector
            link = chain(dve, v_ch)

            def mean_sq(dst, src, n):
                link(V.tensor_scalar(dst, src, 1.0 / n, EPS, ALU.mult, ALU.add))

            dve.wait_ge(silu_e, 1)
            link(V.tensor_scalar_add(cE, cE, 1.0))
            link(V.reciprocal(cE, cE))
            V.tensor_tensor(cT, cT, cE, ALU.mult).then_inc(silu_c, 1)
            dve.wait_ge(u_ps, 1)
            V.tensor_tensor(u_sb, PS[0:NH, 7, 0:UL], line[:, UL:2 * UL], ALU.add).then_inc(u_ok, 1)
            dve.wait_ge(ss_ok, H)
            V.tensor_scalar(rstd, ssum, 1.0 / D, EPS, ALU.mult, ALU.add).then_inc(ms_ok, 1)
            dve.wait_ge(rt_ok, 1)
            link(V.reciprocal(rstd, rstd))
            dve.wait_ge(cst_in, 16)
            for h in range(H):
                V.tensor_scalar(idr[:, h * P:(h + 1) * P], ident, rstd[:, h:h + 1], None, ALU.mult).then_inc(id_ok, 1)
            for i in range(1, KT // 2, 2):
                dve.wait_ge(tr_ps, i + 1)
                V.tensor_copy(hT[:, 2 * i:2 * i + 2, :], PS[:, i % 4, :].rearrange("p (k t) -> p k t", k=2)).then_inc(tr_dve, 1)

            def mod_row(i):
                dve.wait_ge(*((brow1_in, 32) if i < 2 else (brow_in, 16 * (i - 1))))
                if i > 2:
                    dve.wait_ge(mod_out, 16 * (i - 2))
                V.tensor_tensor(mrow, PS[:, 6, :], sq[:, :] if i == 1 else brow, ALU.add).then_inc(mod_ok, 1)

            dve.wait_ge(vec_ps, 1)
            V.tensor_copy(g1goT, PS[:, 5, 0:2 * KT])
            for i in range(2):
                dve.wait_ge(pe_chunk, ADA_CHUNKS * (i + 1))
                mod_row(i)
                dve.wait_ge(mc_ps, i + 1)
                cols = PS[:, 7, :].rearrange("p (j q r) -> p q j r", j=4, q=4)[:, :, :, 0]
                V.tensor_copy((B1, A1)[i].rearrange("p (q j) -> p q j", q=4), cols).then_inc(mc_ok, 1)
            dve.wait_ge(mc_ok, 2)
            V.scalar_tensor_tensor(A1, A1, 1.0, g1T, ALU.add, ALU.mult).then_inc(ab_ok, 1)
            dve.wait_ge(ab_ok, 1)
            dve.wait_ge(tr_act, KT // 4)
            dve.wait_ge(tr_dve, KT // 4)
            for t in range(1, KT, 2):
                V.tensor_scalar(hT[:, t, :], hT[:, t, :], A1[:, t:t + 1], B1[:, t:t + 1], ALU.mult, ALU.add).then_inc(aff_dve, 1)

            ada_n = [0]

            def ada_chunk(pt_, j):
                w = on_ring(dve, "adv", (pt_, j)).rearrange("p (t n) -> p t n", t=2)
                for r in range(2):
                    t = 2 * j + r
                    if t == 0:
                        if pt_ != G1:
                            dve.wait_ge(mod_ps, MADE.index(pt_) - 2)
                        ins = V.tensor_scalar(ada_acc, w[:, 0, :], cT[:, 0:1], None, ALU.mult)
                    else:
                        dve.wait_ge(accd, ada_n[0])
                        ins = V.scalar_tensor_tensor(ada_acc, w[:, r, :], cT[:, t:t + 1], ada_acc, ALU.mult, ALU.add)
                    ins.then_inc(accd, 1)
                    ada_n[0] += 1

            dve.wait_ge(u_out, 16)
            for i, pt_ in enumerate((G1, SH2, SC2)):
                for j in range(ADA_CHUNKS):
                    ada_chunk(pt_, j)
                dve.wait_ge(mod_ps, i + 1)
                mod_row(2 + i)

            def logits(h):
                dve.wait_ge(s_ps, h + 1)
                if h % 16 == 0:
                    n = number["bias", h // 16]
                    dve.wait_ge(landed[n % RING], 16 * (n // RING + 1))
                if h >= 4:
                    dve.wait_ge(pt_ps, h - 3)
                B = slot(number["bias", h // 16] % RING).rearrange("p (h k) -> p h k", h=16)[:, h % 16, :]
                low = sink[:, h:h + 1] if h < NHA else LOW
                V.tensor_tensor_reduce(out=L[:, h % 4, 0:T], in0=PS[:, h % 2, 0:T], in1=B, scale=1.0, scalar=low,
                                       op0=ALU.add, op1=ALU.max, accum_out=nmx[:, h, 0:1])
                V.tensor_tensor_reduce(out=L[:, h % 4, T:384], in0=PS[:, h % 2, T:384], in1=B[:, P:T], scale=1.0,
                                       scalar=low, op0=ALU.add, op1=ALU.max, accum_out=nmx[:, h, 1:2]).then_inc(lg_ok, 1)
                dve.wait_ge(lg_ok, h + 1)
                V.tensor_scalar(nmx[:, h, :], nmx[:, h, :], -1.0, None, ALU.mult).then_inc(nm_ok, 1)

            def normalise(h):
                dve.wait_ge(p_ok, h + 1)
                if h < NHA:
                    link(V.tensor_tensor(psum_[:, h, :], psum_[:, h, :], esink[:, h, :], ALU.add))
                link(V.reciprocal(rden[:, h, :], psum_[:, h, :]))
                V.tensor_scalar(L[:, h % 4, 0:T], L[:, h % 4, 0:T], rden[:, h, 0:1], None, ALU.mult)
                V.tensor_scalar(L[:, h % 4, T:384], L[:, h % 4, T:384], rden[:, h, 1:2], None, ALU.mult).then_inc(pn_ok, 1)

            def y_evac(b):
                dve.wait_ge(y_ps, b + 1)
                V.tensor_copy(yT[:, b, :], PS[:, 4 + b % 2, 0:T]).then_inc(y_ok, 1)

            dve.wait_ge(small_in, 32)
            for h in range(NH + 4):
                if h < NH:
                    logits(h)
                if 1 <= h <= NH:
                    normalise(h - 1)
                if h >= 5 and h % 2 == 1:
                    y_evac((h - 5) // 2)
            dve.wait_ge(yss_ps, NH // 2)
            for i in range(2):
                ins = V.tensor_scalar(sq[:, i * T:(i + 1) * T], PS[:, 6 + i, 0:T], 1.0 / (NHA * HD), EPS, ALU.mult, ALU.add)
            ins.then_inc(yms_ok, 1)
            dve.wait_ge(yrt_ok, 1)
            link(V.reciprocal(sq[:, :], sq[:, :]))
            dve.wait_ge(y_ok, NH // 2)
            for b in range(KT):
                i = b // (KT // 2)
                V.scalar_tensor_tensor(yT[:, b, :], yT[:, b, :], goT[:, b:b + 1], sq[:, i * T:(i + 1) * T],
                                       ALU.mult, ALU.mult).then_inc(yn_ok, 1)
            gyv = gy[:, :].rearrange("p (h n) -> p h n", h=H)
            for cc in range(WO_CHUNKS):
                dve.wait_ge(pe_chunk, 2 * ADA_CHUNKS + QKV_CHUNKS + cc + 1)
                if cc == 0:
                    dve.wait_ge(xr_ok, 1)
                    dve.wait_ge(mod_in, 16 * 3)
                cols = slice(cc * CW, (cc + 1) * CW)
                gb = g1b[:, cols].unsqueeze(1).to_broadcast([P, H, CW])
                link(V.tensor_tensor(gyv, PS[:, cc % 4, :].rearrange("p (h n) -> p h n", h=H), gb, ALU.mult))
                ins = V.tensor_tensor(x1[:, :, cols], x1[:, :, cols], gyv, ALU.add)
                ins.then_inc(x1_ok, 1)
                ada_chunk(G2, cc)
            dve.wait_ge(x1_ss, WO_CHUNKS)
            link(V.reduce_sum(ssum, part, axis=AX.X))
            V.tensor_scalar(rstd, ssum, 1.0 / D, EPS, ALU.mult, ALU.add).then_inc(ms_ok, 1)
            dve.wait_ge(rt_ok, 2)
            link(V.reciprocal(rstd, rstd))
            for h in range(H):
                V.tensor_scalar(idr[:, h * P:(h + 1) * P], ident, rstd[:, h:h + 1], None, ALU.mult).then_inc(id_ok, 1)
            dve.wait_ge(mod_in, 16 * 3)
            V.scalar_tensor_tensor(A2, A2, 1.0, g2T, ALU.add, ALU.mult).then_inc(ab_ok, 1)
            dve.wait_ge(ab_ok, 2)
            for i in range(1, KT // 2, 2):
                dve.wait_ge(tr_ps, KT // 2 + i + 1)
                for t in (2 * i, 2 * i + 1):
                    last = V.tensor_scalar(h2T[:, t, :], PS[:, i % 4, t % 2 * T:(t % 2 + 1) * T], A2[:, t:t + 1],
                                           B2[:, t:t + 1], ALU.mult, ALU.add)
                last.then_inc(tr_dve, 1)
            dve.wait_ge(mod_ps, 4)
            mod_row(5)
            link(V.memset(posx[:, :, E:E + 4], -1.0))
            link(V.memset(gatex[:, :, E:E + 4], 0.0))
            dve.wait_ge(rw_in, 64)
            dve.wait_ge(rt_ps, 1)
            dve.wait_ge(mod_out, 16 * 4)
            link(V.tensor_tensor(R_lg, PS[:, 5, 0:H * NR].rearrange("p (h n) -> p h n", h=H),
                                 rb.unsqueeze(1).to_broadcast([P, H, NR]), ALU.add))

            def first_largest(dst, val, desc, n, top, tmp):
                link(V.reduce_max(top, val, axis=AX.X))
                link(V.tensor_tensor(tmp, val, top.unsqueeze(2).to_broadcast([P, H, n]), ALU.is_equal))
                link(V.tensor_tensor(tmp, tmp, desc.unsqueeze(1).to_broadcast([P, H, n]), ALU.mult))
                link(V.reduce_max(R_m, tmp, axis=AX.X))
                link(V.tensor_tensor(dst, tmp, R_m.unsqueeze(2).to_broadcast([P, H, n]), ALU.is_equal))

            grp = R_lg[:, :, 0:G]
            first_largest(R_goh, grp, cst[:, C_DG:C_DG + G], G, R_gm, R_t4)
            V.tensor_tensor(R_ge, grp, R_gm.unsqueeze(2).to_broadcast([P, H, G]), ALU.subtract).then_inc(ge_in, 1)
            for h in range(H):
                link(V.tensor_tensor(R_x[:, h], R_lg[:, h, G:NR].rearrange("p (g e) -> p g e", g=G),
                                     R_goh[:, h].unsqueeze(2).to_broadcast([P, G, EPG]), ALU.mult))
                link(V.reduce_sum(R_in[:, h], R_x[:, h].rearrange("p g e -> p e g"), axis=AX.X))
            desc = cst[:, C_DE:C_DE + EPG]
            first_largest(R_o1, R_in, desc, EPG, R_v1, R_t8)
            link(V.scalar_tensor_tensor(R_in2, R_o1, LOW, R_in, ALU.mult, ALU.add))
            first_largest(R_o2, R_in2, desc, EPG, R_v2, R_t8)
            V.tensor_tensor(R_e2, R_v2, R_v1, ALU.subtract).then_inc(e2_in, 1)
            link(V.tensor_tensor(R_t8, R_o1, R_o2, ALU.add))

            def by_group(dst, val):
                for h in range(H):
                    ins = V.tensor_tensor(dst[:, h].rearrange("p (g e) -> p g e", g=G),
                                          R_goh[:, h].unsqueeze(2).to_broadcast([P, G, EPG]),
                                          val[:, h].unsqueeze(1).to_broadcast([P, G, EPG]), ALU.mult)
                return ins
            by_group(R_mem, R_t8).then_inc(mem_ok, 1)
            dve.wait_ge(ge_ok, 1)
            link(V.reduce_sum(R_gm, R_ge, axis=AX.X))
            link(V.reciprocal(R_gm, R_gm))
            dve.wait_ge(e2_ok, 1)
            link(V.tensor_scalar_add(R_w1, R_e2, 1.0))
            link(V.reciprocal(R_w1, R_w1))
            link(V.tensor_tensor(R_w1, R_w1, R_gm, ALU.mult))
            link(V.tensor_tensor(R_e2, R_e2, R_w1, ALU.mult))
            link(V.tensor_tensor(R_o1, R_o1, R_w1.unsqueeze(2).to_broadcast([P, H, EPG]), ALU.mult))
            link(V.tensor_tensor(R_o2, R_o2, R_e2.unsqueeze(2).to_broadcast([P, H, EPG]), ALU.mult))
            link(V.tensor_tensor(R_o1, R_o1, R_o2, ALU.add))
            link(by_group(gates, R_o1))
            dve.wait_ge(pos_ps, 1)
            link(V.scalar_tensor_tensor(posm, PS[:, 7, 0:H * E].rearrange("p (h e) -> p h e", h=H), 1.0, R_mem,
                                        ALU.add, ALU.mult))
            link(V.tensor_scalar(posm, posm, -1.0, None, ALU.add))
            link(V.scalar_tensor_tensor(over, posm, float(SLOTS), gates, ALU.is_ge, ALU.mult))
            link(V.reduce_max(R_m[:, 0:1], PS[:, 7, H * E:(H + 1) * E], axis=AX.X))
            link(V.tensor_scalar(R_m[:, 1:2], R_m[:, 0:1], float(SLOTS), None, ALU.is_gt))
            V.tensor_copy(ovi[:, :], R_m[:, 1:2]).then_inc(routed, 1)
            dve.wait_ge(routed, 1)

            def build_sel(g):
                shape = [P, 4, SLOTS]
                for h in range(H):
                    pos4 = posx[:, h, bass.ds(4 * g, 4)].unsqueeze(2).to_broadcast(shape)
                    V.tensor_tensor(EQ[:, h].rearrange("p (e s) -> p e s", e=4), pos4,
                                    iota.unsqueeze(1).to_broadcast(shape), ALU.is_equal).then_inc(eq_ok, 1)
                dve.wait_ge(eq_ok, 2 * g + 2)
                for h in range(H):
                    gt4 = gatex[:, h, bass.ds(4 * g, 4)].unsqueeze(2).to_broadcast(shape)
                    V.tensor_scalar(selr[:, h], EQ[:, h], rstd[:, h:h + 1], None, ALU.mult).then_inc(sel_ok, 1)
                    V.tensor_tensor(selg[:, h].rearrange("p (e s) -> p e s", e=4),
                                    EQ[:, h].rearrange("p (e s) -> p e s", e=4), gt4, ALU.mult).then_inc(sel_ok, 1)

            def acc_add(p):
                for k in range(2 * 4):
                    h, ch = k // 4, k % 4
                    dve.wait_ge(sc_ps, 8 * p + k + 1)
                    a = acc[:, h, 512 * ch:512 * ch + 512]
                    V.tensor_tensor(a, a, PS[:, 6 + k % 2, :], ALU.add).then_inc(acc_ok, 1)

            def silu_up(g, i):
                dve.wait_ge(ex_ok, 4 * g + i + 1)
                V.tensor_scalar_add(den, ex, 1.0).then_inc(silu_st, 1)
                dve.wait_ge(silu_st, 12 * g + 3 * i + 1)
                V.reciprocal(rc, den).then_inc(silu_st, 1)
                dve.wait_ge(silu_st, 12 * g + 3 * i + 2)
                V.tensor_tensor(sg, rc, PS[:, i % 2, 0:T], ALU.mult).then_inc(silu_st, 1)
                dve.wait_ge(silu_st, 12 * g + 3 * i + 3)
                if i:
                    dve.wait_ge(hd_ps, 4 * g + i)
                V.tensor_tensor(hid, sg, PS[:, i % 2, T:2 * T], ALU.mult).then_inc(hid_ok, 1)

            def result(g, i):
                dve.wait_ge(pe_chunk, PE0 + 24 * g + DN_END[i])
                if i == 0:
                    dve.wait_ge(fin_in, 16)
                ydv = yd.rearrange("p (i q n) -> p i q n", i=2, q=2)
                g2v = g2b.rearrange("p (i q n) -> p i q n", i=2, q=2)
                for q in range(2):
                    rows = slice(64 * q, 64 * q + 64)
                    V.tensor_tensor(ydv[64 * (i % 2):64 * (i % 2) + 64, :, q, :], PS[rows, 4:6, :],
                                    g2v[rows, :, q, :], ALU.mult).then_inc(yd_ok, 1)

            build_sel(0)
            with dve.Fori(0, E // 4) as g:
                for i in range(1, KT // 2, 2):
                    dve.wait_ge(ga_ps, 8 * g + i + 1)
                    for t in (2 * i, 2 * i + 1):
                        last = V.tensor_scalar(hT[:, t, :], PS[:, 3, t % 2 * T:(t % 2 + 1) * T], A2[:, t:t + 1],
                                               B2[:, t:t + 1], ALU.mult, ALU.add)
                    last.then_inc(hg_dve, 1)
                silu_up(g, 0)
                silu_up(g, 1)
                result(g, 0)
                silu_up(g, 2)
                result(g, 1)
                acc_add(2 * g)
                silu_up(g, 3)
                result(g, 2)
                dve.wait_ge(st_ps, 2 * g + 2)
                build_sel(g + 1)
                result(g, 3)
                acc_add(2 * g + 1)

            n_over = dve.value_load(ovi[0:1, 0:1], min_val=0, max_val=1)
            with dve.If(n_over > 0):
                for i in range(KT // 2):
                    dve.wait_ge(fb_hps, i + 1)
                    for r in range(2):
                        t = 2 * i + r
                        V.tensor_scalar(F_h[:, t, :], PS[:, 3 + i % 2, r * T:(r + 1) * T], A2[:, t:t + 1],
                                        B2[:, t:t + 1], ALU.mult, ALU.add).then_inc(fb_ht, 1)
                with dve.Fori(0, E) as e:
                    for h in range(H):
                        dve.wait_ge(fb_ex, 2 * e + h + 1)
                        V.tensor_scalar_add(F_ex, F_ex, 1.0).then_inc(fb_link, 1)
                        dve.wait_ge(fb_link, 6 * e + 3 * h + 1)
                        V.reciprocal(F_ex, F_ex).then_inc(fb_link, 1)
                        dve.wait_ge(fb_link, 6 * e + 3 * h + 2)
                        V.tensor_tensor(F_ex, F_ex, PS[:, 0, :], ALU.mult).then_inc(fb_link, 1)
                        dve.wait_ge(fb_link, 6 * e + 3 * h + 3)
                        V.tensor_tensor(F_hid, F_ex, PS[:, 1, :], ALU.mult).then_inc(fb_hid, 1)
                        for ch in range(4):
                            dve.wait_ge(fb_dn, 8 * e + 4 * h + ch + 2)
                            a = acc[:, h, 512 * ch:512 * ch + 512]
                            V.tensor_tensor(F_y, PS[:, 3 + ch, :], g2b[:, 512 * ch:512 * ch + 512],
                                            ALU.mult).then_inc(fb_y, 1)
                            dve.wait_ge(fb_y, 8 * e + 4 * h + ch + 1)
                            V.scalar_tensor_tensor(a, F_y, over[:, h, bass.ds(e, 1)], a,
                                                   ALU.mult, ALU.add).then_inc(fb_acc, 1)
                            dve.wait_ge(fb_acc, 8 * e + 4 * h + ch + 1)
                dve.wait_ge(fb_acc, 8 * E)
            dve.wait_ge(fg_in, 16)
            for h in range(H):
                dve.wait_ge(f_ms, 4 * h + 4)
                link(V.reduce_sum(ssum[:, h:h + 1], part[:, h, 0:4], axis=AX.X))
                V.tensor_scalar(rstd[:, h:h + 1], ssum[:, h:h + 1], 1.0 / D, EPS, ALU.mult, ALU.add).then_inc(f_rt, 1)
                dve.wait_ge(f_r, h + 1)
                link(V.reciprocal(rstd[:, h:h + 1], rstd[:, h:h + 1]))
                for n0 in (0, D // 2):
                    a = acc[:, h, n0:n0 + D // 2]
                    V.scalar_tensor_tensor(a, a, rstd[:, h:h + 1], fgb[:, n0:n0 + D // 2], ALU.mult, ALU.mult).then_inc(o_ok, 1)

        @block.tensor
        def _(pe):
            mm = nc.tensor.matmul
            pe.wait_ge(line_in, 32)
            mm(PS[0:NH, 7, 0:UL], relb, line[:, 0:UL], start=True, stop=True).then_inc(u_ps, 1)

            def transposes(rows, done_act, done_dve):
                for i in range(KT // 2):
                    if i >= 4:
                        pe.wait_ge(tr_act, done_act(i - 4))
                        if done_dve(i - 4):
                            pe.wait_ge(tr_dve, done_dve(i - 4))
                    for r in range(2):
                        for h in range(H):
                            last = mm(PS[:, i % 4, r * T + h * P:r * T + (h + 1) * P],
                                      rows(h, 2 * i + r), idr[:, h * P:(h + 1) * P],
                                      start=True, stop=True)
                    last.then_inc(tr_ps, 1)

            pe.wait_ge(vrow_in, 48)
            pe.wait_ge(cst_in, 16)
            mm(PS[:, 5, 0:2 * KT], vrow[0:2 * KT, :], ident[0:2 * KT, 0:2 * KT], start=True, stop=True).then_inc(vec_ps, 1)
            pe.wait_ge(id_ok, H)
            pe.wait_ge(x_in, 16)
            transposes(lambda h, t: x1[:, h, t * P:(t + 1) * P], lambda i: (i + 2) // 2, lambda i: (i + 1) // 2)
            pe.wait_ge(silu_c, 1)
            with pe.Fori(0, 2) as i:
                for j in range(ADA_CHUNKS):
                    pe.wait_ge(landed[j], 16 * i + 16)
                    w = slot(j).rearrange("p (t n) -> p t n", t=2)
                    for r in range(2):
                        for q in range(4):
                            last = mm(PS[32 * q:32 * q + 32, 6, :], cT[:, 2 * j + r:2 * j + r + 1].to_broadcast([P, 32]),
                                      w[:, r, 512 * q:512 * q + 512], start=(j + r == 0), stop=(j + r == ADA_CHUNKS))
                    last.then_inc(pe_chunk, 1)
                pe.wait_ge(mod_ok, i + 1)
                for j in range(4):
                    last = nc.tensor.transpose(PS[:, 7, j * P:(j + 1) * P], mrow[:, j * P:(j + 1) * P], ident)
                last.then_inc(mc_ps, 1)

            def sum_part(i):
                pe.wait_ge(accd, 2 * ADA_CHUNKS * (i + 1))
                pe.wait_ge(mod_ok, 2 + i)
                for q in range(4):
                    last = mm(PS[32 * q:32 * q + 32, 6, :], ones[:, 0:32], ada_acc[:, 512 * q:512 * q + 512],
                              start=True, stop=True)
                last.then_inc(mod_ps, 1)

            n_sum = 0
            for cc in range(QKV_CHUNKS):
                w = on_ring(pe, "qkv", cc).rearrange("p (t n) -> p t n", t=KT)
                if cc >= 4:
                    pe.wait_ge(qkv_ok, cc - 3)
                ps = PS[:, cc % 4, :]
                for sub in range(2):
                    if cc < BV and not (cc == NQ and sub == 1):
                        for t in range(KT):
                            if cc == 0 and sub == 0:
                                pe.wait_ge((aff_act, aff_dve)[t % 2], t // 2 + 1)
                            last = mm(ps[:, sub * T:(sub + 1) * T], w[:, t, sub * P:(sub + 1) * P], hT[:, t, :],
                                      start=(t == 0), stop=(t == KT - 1))
                    elif cc == NQ:
                        for h in range(H):
                            for t in range(KT):
                                last = mm(ps[:, T + h * P:T + (h + 1) * P], hT[:, t, h * P:(h + 1) * P], w[:, t, P:2 * P],
                                          start=(t == 0), stop=(t == KT - 1))
                    else:
                        for t in range(KT):
                            last = mm(ps[:, sub * CW:(sub + 1) * CW], hT[:, t, sub * P:(sub + 1) * P], w[:, t, :],
                                      start=(t == 0), stop=(t == KT - 1))
                last.then_inc(pe_chunk, 1)
                for _ in SUM_AFTER.get(cc, ()):
                    sum_part(n_sum)
                    n_sum += 1

            pe.wait_ge(qkv_ok, QKV_CHUNKS)

            def scores(h):
                if h >= 2:
                    pe.wait_ge(lg_ok, h - 1)
                k = kTa[:, 2 * (h // (NHA // KVA)) + h % 2, :] if h < NHA else kTb[:, h - NHA, :]
                mm(PS[:, h % 2, 0:T], qT[:, h // 2, P:T], k, start=True, stop=True)
                mm(PS[:, h % 2, T:384], qT[:, h // 2, 0:P], k[:, 0:P], start=True, stop=True).then_inc(s_ps, 1)

            def transpose_p(h):
                pe.wait_ge(pn_ok, h + 1)
                if h >= 2:
                    pe.wait_ge(pt_ok, h - 1)
                for k in range(3):
                    last = nc.tensor.transpose(PS[:, 2 + h % 2, k * P:(k + 1) * P], L[:, h % 4, k * P:(k + 1) * P], rev)
                last.then_inc(pt_ps, 1)

            def values(b):
                pe.wait_ge(pt_ok, 2 * b + 2)
                if b >= 2:
                    pe.wait_ge(y_ok, b - 1)
                for (q0, pk, half, st, sp_) in ((P, 0, 0, True, False), (P, 1, 1, False, True), (0, 2, 0, True, True)):
                    for r in range(2):
                        h = 2 * b + r
                        n0 = (h // (NHA // KVA)) * HD if h < NHA else KVA * HD + (h - NHA) * HD
                        last = mm(PS[64 * r:64 * r + 64, 4 + b % 2, q0:q0 + P], v_sb[:, half, n0:n0 + HD],
                                  PT[:, h % 4, pk * P:(pk + 1) * P], start=st, stop=sp_)
                last.then_inc(y_ps, 1)

            def square_sums(b):
                pe.wait_ge(sq_ok, b + 1)
                i, n = divmod(b, KT // 2)
                mm(PS[:, 6 + i, 0:T], ones, sq[:, b % 2 * T:(b % 2 + 1) * T], start=(n == 0),
                   stop=(n == KT // 2 - 1)).then_inc(yss_ps, 1)

            pe.wait_ge(mod_ok, 5)
            for h in range(NH + 5):
                if h < NH:
                    scores(h)
                if 2 <= h < NH + 2:
                    transpose_p(h - 2)
                if 4 <= h < NH + 4 and h % 2 == 0:
                    values((h - 4) // 2)
                if h >= 6 and h % 2 == 0:
                    square_sums((h - 6) // 2)
            for cc in range(WO_CHUNKS):
                w = on_ring(pe, "wo", cc).rearrange("p (t n) -> p t n", t=KT)
                if cc >= 4:
                    pe.wait_ge(x1_ok, cc - 3)
                for h in range(H):
                    for t in range(KT):
                        if cc == 0 and h == 0:
                            pe.wait_ge(yn_ok, t + 1)
                        last = mm(PS[:, cc % 4, h * CW:(h + 1) * CW], yT[:, t, h * P:(h + 1) * P], w[:, t, :],
                                  start=(t == 0), stop=(t == KT - 1))
                last.then_inc(pe_chunk, 1)
            pe.wait_ge(id_ok, 2 * H)
            pe.wait_ge(x1_ok, WO_CHUNKS)
            transposes(lambda h, t: x1[:, h, t::KT], lambda i: KT // 4 + (i + 2) // 2, lambda i: KT // 4 + (i + 1) // 2)
            pe.wait_ge(rw_in, 64)
            for t in range(KT):
                pe.wait_ge((tr_act, tr_dve)[t // 2 % 2], KT // 4 + t // 4 + 1)
                last = mm(PS[0:NR, 4, 0:T], wr[:, t, :], h2T[:, t, :], start=(t == 0), stop=(t == KT - 1))
            last.then_inc(rl_ps, 1)
            sum_part(3)
            pe.wait_ge(rl_ok, 1)
            for h in range(H):
                last = mm(PS[:, 5, h * NR:(h + 1) * NR], lgT[:, h * P:(h + 1) * P], ident[0:NR, 0:NR], start=True, stop=True)
            last.then_inc(rt_ps, 1)
            pe.wait_ge(mem_ok, 1)
            mm(PS[:, 7, 0:E], tri, R_mem[:, 0], start=True, stop=True)
            mm(PS[:, 7, E:2 * E], tri, R_mem[:, 1], start=True, stop=False)
            mm(PS[:, 7, E:2 * E], ones, R_mem[:, 0], start=False, stop=True)
            mm(PS[:, 7, 2 * E:3 * E], ones, R_mem[:, 0], start=True, stop=False)
            mm(PS[:, 7, 2 * E:3 * E], ones, R_mem[:, 1], start=False, stop=True).then_inc(pos_ps, 1)

            pe.wait_ge(routed, 1)

            def chunk_at(g, m):
                s = (S0 + m) % RING
                pe.wait_ge(landed[s], 16 * (N0 // RING + 1 + (S0 + m) // RING) + 48 * g)
                return s

            def scatter(p):
                pe.wait_ge(selT_ok, p + 1)
                pe.wait_ge(yd_ok, 4 * p + 4)
                for k in range(8):
                    h, ch = k // 4, k % 4
                    pe.wait_ge(acc_ok, 8 * p + max(1, k))
                    mm(PS[:, 6 + k % 2, :], selT[:, h * P:(h + 1) * P], yd[:, 512 * ch:512 * ch + 512],
                       start=True, stop=True).then_inc(sc_ps, 1)

            def sel_transpose(p, pi):
                for h in range(H):
                    last = nc.tensor.transpose(PS[:, 2, h * P:(h + 1) * P], selg[:, h, pi * P:(pi + 1) * P], ident)
                last.then_inc(st_ps, 1)

            with pe.Fori(0, E // 4) as g:
                pe.wait_ge(sel_ok, 4 * g + 4)
                for i in range(KT // 2):
                    if i >= 2:
                        pe.wait_ge((hg_act, hg_dve)[i % 2], 4 * g + i // 2)
                    for r in range(2):
                        for h in range(H):
                            last = mm(PS[:, 2 + i % 2, r * T:(r + 1) * T], x1[:, h, 2 * i + r::KT], selr[:, h],
                                      start=(h == 0), stop=(h == H - 1))
                    last.then_inc(ga_ps, 1)
                pe.wait_ge(hg_act, 4 * g + 4)
                pe.wait_ge(hg_dve, 4 * g + 4)
                def gate_up(i):
                    for half in range(2):
                        s = chunk_at(g, GU_AT[i] + 2 * half)
                        chunk_at(g, GU_AT[i] + 2 * half + 1)
                        w = ring[:, s * SLOT:(s + 2) * SLOT].rearrange("p (m t n) -> p m t n", m=2, n=FE)
                        for t in range(KT // 2):
                            k = half * (KT // 2) + t
                            for j in range(2):
                                last = mm(PS[64 * j:64 * j + 64, i % 2, :].rearrange("p (m n) -> p m n", m=2),
                                          hT[:, k, i * SLOTS:(i + 1) * SLOTS], w[:, :, t, 256 * j:256 * j + 256],
                                          start=(k == 0), stop=(k == KT - 1))
                        last.then_inc(pe_chunk, 2)

                def hid_transpose(i):
                    pe.wait_ge(hid_ok, 4 * g + i + 1)
                    for b in range(2):
                        last = nc.tensor.transpose(PS[:, 3, b * P:(b + 1) * P], hid[:, b * P:(b + 1) * P], ident)
                    last.then_inc(hd_ps, 1)

                def down(i):
                    pe.wait_ge(hidT_ok, 4 * g + i + 1)
                    if i % 2:
                        pe.wait_ge(yd_ok, 8 * g + 2 * i)
                    for j in range(2):
                        w = slot(chunk_at(g, DN_AT[i] + j)).rearrange("p (b n) -> p b n", b=2)
                        for b in range(2):
                            for i2 in range(2):
                                for q in range(2):
                                    ch = 2 * i2 + q
                                    last = mm(PS[64 * q:64 * q + 64, 4 + i2, :], hidT[:, b, 64 * j:64 * j + 64],
                                              w[:, b, 512 * ch:512 * ch + 512], start=(j + b == 0), stop=(j + b == 2))
                        last.then_inc(pe_chunk, 1)

                gate_up(0)
                sel_transpose(2 * g, 0)
                gate_up(1)
                hid_transpose(0)
                down(0)
                gate_up(2)
                hid_transpose(1)
                down(1)
                gate_up(3)
                hid_transpose(2)
                scatter(2 * g)
                sel_transpose(2 * g + 1, 1)
                down(2)
                hid_transpose(3)
                down(3)
                scatter(2 * g + 1)

            n_over = pe.value_load(ovi[0:1, 0:1], min_val=0, max_val=1)
            with pe.If(n_over > 0):
                pe.wait_ge(acc_ok, 8 * E // 2 + 1)
                for i in range(KT // 2):
                    if i >= 2:
                        pe.wait_ge(fb_ht, 2 * (i - 1))
                    for r in range(2):
                        for h in range(H):
                            last = mm(PS[:, 3 + i % 2, r * T + h * P:r * T + (h + 1) * P], x1[:, h, 2 * i + r::KT],
                                      idr[:, h * P:(h + 1) * P], start=True, stop=True)
                    last.then_inc(fb_hps, 1)
                pe.wait_ge(fb_ht, KT)
                pe.sem_inc(fb_dn, 1)
                with pe.Fori(0, E) as e:
                    pe.wait_ge(fb_in, 96 * e + 96)
                    for h in range(H):
                        for m in range(2):
                            for t in range(KT):
                                w = slot(2 * (t // 8) + m).rearrange("p (t n) -> p t n", n=FE)
                                last = mm(PS[:, m, :], F_h[:, t, h * P:(h + 1) * P], w[:, t % 8, :],
                                          start=(t == 0), stop=(t == KT - 1))
                        last.then_inc(fb_up, 1)
                        pe.wait_ge(fb_hid, 2 * e + h + 1)
                        for k in range(4):
                            last = nc.tensor.transpose(PS[:, 2, k * P:(k + 1) * P], F_hid[:, k * P:(k + 1) * P], ident)
                        last.then_inc(fb_tps, 1)
                        pe.wait_ge(fb_tok, 2 * e + h + 1)
                        for ch in range(4):
                            for k in range(4):
                                w = slot(4 + k // 2).rearrange("p (b n) -> p b n", b=2)
                                last = mm(PS[:, 3 + ch, :], F_hT[:, k * P:(k + 1) * P],
                                          w[:, k % 2, 512 * ch:512 * ch + 512], start=(k == 0), stop=(k == 3))
                            last.then_inc(fb_dn, 1)
                        pe.wait_ge(fb_acc, 8 * e + 4 * h + 4)


_INS = ['x', 'c', 'rel_bias', 'w_ada', 'b_ada', 'norm1_g', 'norm2_g', 'w_qkv', 'attn_sinks', 'swa_out_g',
        'moba_out_g', 'w_o', 'w_group', 'b_group', 'w_expert_router', 'b_expert_router', 'w_gate', 'w_up',
        'w_down', 'final_g']


def kernel(**inputs):
    import numpy as _np
    import concourse.bacc as _bacc
    from concourse import mybir as _mybir
    from concourse.bass_utils import run_bass_kernel_spmd as _run

    nc = _bacc.Bacc("TRN2", target_bir_lowering=False, num_devices=1, dynamic_dma_scratch_size=8192)
    table, lines = constants()
    arrays, args = {}, []
    for name in _INS:
        arrays[f"in_{name}"] = _np.ascontiguousarray(inputs[name])
    arrays["const_table"], arrays["const_lines"] = table, lines
    for name, a in arrays.items():
        args.append(nc.dram_tensor(name, a.shape, _mybir.dt.from_np(a.dtype), kind="ExternalInput").ap())
    shape = arrays["in_x"].shape
    args.append(nc.dram_tensor("out_0", shape, _mybir.dt.float32, kind="ExternalOutput").ap())
    layer_kernel(nc, *args)
    r = _run(nc, [arrays], core_ids=[0])
    return r.results[0]["out_0"]
```
